# Optimizing a Trainium2 kernel written in Bass

```python
import jax, jax.numpy as jnp
from jax import lax
import numpy as np

D_MODEL = 1024
BATCH = 1
SEQ = 512
DEPTH = 2

GRID_W = 64
CTX_LEN = 256
EPS = 1e-6
ROPE_BASE = 10000.0
Q_BLOCK = 128
NEG_INF = -1e30

A_HEADS = 4
A_NOPE = 128
A_ROPE = 64
A_V = 128
A_Q_RANK = 256
A_KV_RANK = 128
B_HEADS = 8
B_KV_HEADS = 2
B_HD = 64
WINDOW = 128
C_HEADS = 4
C_DK = 64
C_DV = 128
C_DECAY_RANK = 16
C_DECAY_TEMP = 16.0
C_CHUNK = 64
D_HEADS = 4
D_KV_HEADS = 2
D_HD = 128
N_BRANCH = 4
BRANCH_W = 512
D_FF = 4 * D_MODEL

A_COLS = A_Q_RANK + A_KV_RANK + A_ROPE
B_COLS = (B_HEADS + 2 * B_KV_HEADS) * B_HD
C_COLS = 2 * C_HEADS * C_DK + 2 * C_HEADS * C_DV + 2 * C_DECAY_RANK
D_COLS = (D_HEADS + 2 * D_KV_HEADS) * D_HD
GATE_COLS = N_BRANCH * D_MODEL
IN_SPLITS = (A_COLS, B_COLS, C_COLS, D_COLS, GATE_COLS)
IN_COLS = A_COLS + B_COLS + C_COLS + D_COLS + GATE_COLS

kernel_name = 'hybrid_parallel_mixer_flow_block'

def rmsnorm(x, w):
    xf = x.astype(jnp.float32)
    y = xf * lax.rsqrt(jnp.mean(xf * xf, axis=-1, keepdims=True) + EPS)
    return (y * w.astype(jnp.float32)).astype(x.dtype)

def modulate(h, shift, scale):
    return h * (1 + scale) + shift

def split_cols(t, sizes):
    return jnp.split(t, [int(s) for s in np.cumsum(sizes)[:-1]], axis=-1)

def to_heads(t, n, d):
    b, l, _ = t.shape
    return t.reshape(b, l, n, d).transpose(0, 2, 1, 3)

def from_heads(t):
    b, h, l, d = t.shape
    return t.transpose(0, 2, 1, 3).reshape(b, l, h * d)

def rope_1d(x, pos):
    half = x.shape[-1] // 2
    inv = ROPE_BASE ** (-jnp.arange(half, dtype=jnp.float32) / half)
    ang = pos.astype(jnp.float32)[:, None] * inv[None, :]
    cos = jnp.cos(ang).astype(x.dtype)
    sin = jnp.sin(ang).astype(x.dtype)
    x1, x2 = x[..., :half], x[..., half:]
    return jnp.concatenate([x1 * cos - x2 * sin, x1 * sin + x2 * cos], axis=-1)

def rope_2d(x, rows, cols):
    half = x.shape[-1] // 2
    return jnp.concatenate([rope_1d(x[..., :half], rows), rope_1d(x[..., half:], cols)], axis=-1)

def dense_block_attention(q, k, v, scale):
    b, hk, g, l, dk = q.shape
    nb = l // Q_BLOCK
    qb = q.reshape(b, hk, g, nb, Q_BLOCK, dk).transpose(3, 0, 1, 2, 4, 5)

    def one_block(qi):
        s = jnp.einsum('bhgqd,bhkd->bhgqk', qi, k).astype(jnp.float32) * scale
        p = jax.nn.softmax(s, axis=-1).astype(v.dtype)
        return jnp.einsum('bhgqk,bhkd->bhgqd', p, v)

    o = lax.map(one_block, qb)
    return o.transpose(1, 2, 3, 0, 4, 5).reshape(b, hk, g, l, v.shape[-1])

def mla_mixer(p_lat, p_ctx, q_norm_w, w_uq, kv_norm_w, w_ukv, rows, cols, need_ctx):
    def project(p, rope):
        c_q, c_kv, k_rope = split_cols(p, [A_Q_RANK, A_KV_RANK, A_ROPE])
        q = to_heads(rmsnorm(c_q, q_norm_w) @ w_uq, A_HEADS, A_NOPE + A_ROPE)
        kv = to_heads(rmsnorm(c_kv, kv_norm_w) @ w_ukv, A_HEADS, A_NOPE + A_V)
        q_nope, q_rope = q[..., :A_NOPE], q[..., A_NOPE:]
        k_nope, v = kv[..., :A_NOPE], kv[..., A_NOPE:]
        k_rope = k_rope[:, None]
        if rope:
            q_rope = rope_2d(q_rope, rows, cols)
            k_rope = rope_2d(k_rope, rows, cols)
        k_rope = jnp.broadcast_to(k_rope, k_nope.shape[:-1] + (A_ROPE,))
        q = jnp.concatenate([q_nope, q_rope], axis=-1)[:, :, None]
        k = jnp.concatenate([k_nope, k_rope], axis=-1)
        return q, k, v

    scale = (A_NOPE + A_ROPE) ** -0.5
    q, k, v = project(p_lat, True)
    qc, kc, vc = project(p_ctx, False)
    y = dense_block_attention(q, jnp.concatenate([kc, k], axis=2), jnp.concatenate([vc, v], axis=2), scale)
    y_lat = from_heads(y[:, :, 0])
    y_ctx = from_heads(dense_block_attention(qc, kc, vc, scale)[:, :, 0]) if need_ctx else None
    return y_lat, y_ctx

def window_sink_mixer(p_lat, p_ctx, sink, rows, cols, need_ctx):
    g = B_HEADS // B_KV_HEADS
    scale = B_HD ** -0.5

    def project(p, rope):
        q, k, v = split_cols(p, [B_HEADS * B_HD, B_KV_HEADS * B_HD, B_KV_HEADS * B_HD])
        q, k, v = to_heads(q, B_HEADS, B_HD), to_heads(k, B_KV_HEADS, B_HD), to_heads(v, B_KV_HEADS, B_HD)
        if rope:
            q, k = rope_2d(q, rows, cols), rope_2d(k, rows, cols)
        b, _, l, _ = q.shape
        return q.reshape(b, B_KV_HEADS, g, l, B_HD), k, v

    q, k, v = project(p_lat, True)
    qc, kc, vc = project(p_ctx, False)
    sink_f = sink.astype(jnp.float32).reshape(B_KV_HEADS, g)
    n_ctx = kc.shape[2]
    b, hk, _, t, d = q.shape
    nb = t // Q_BLOCK
    qb = q.reshape(b, hk, g, nb, Q_BLOCK, d)

    def bands(z):
        zp = jnp.pad(z, ((0, 0), (0, 0), (Q_BLOCK, Q_BLOCK), (0, 0)))
        return jnp.concatenate(
            [zp[:, :, j * Q_BLOCK: j * Q_BLOCK + t].reshape(b, hk, nb, Q_BLOCK, d) for j in range(3)], axis=3)

    kb, vb = bands(k), bands(v)
    qpos = jnp.arange(nb)[:, None] * Q_BLOCK + jnp.arange(Q_BLOCK)[None, :]
    kpos = jnp.arange(nb)[:, None] * Q_BLOCK - Q_BLOCK + jnp.arange(3 * Q_BLOCK)[None, :]
    valid = ((kpos[:, None, :] >= 0) & (kpos[:, None, :] < t)
             & (jnp.abs(qpos[:, :, None] - kpos[:, None, :]) <= WINDOW))
    s_loc = jnp.where(valid, jnp.einsum('bhgnqd,bhnkd->bhgnqk', qb, kb).astype(jnp.float32) * scale, NEG_INF)
    s_ctx = jnp.einsum('bhgnqd,bhcd->bhgnqc', qb, kc).astype(jnp.float32) * scale
    s_sink = jnp.broadcast_to(sink_f[None, :, :, None, None, None], s_loc.shape[:-1] + (1,))
    pr = jax.nn.softmax(jnp.concatenate([s_ctx, s_loc, s_sink], axis=-1), axis=-1).astype(v.dtype)
    o = (jnp.einsum('bhgnqc,bhcd->bhgnqd', pr[..., :n_ctx], vc)
         + jnp.einsum('bhgnqk,bhnkd->bhgnqd', pr[..., n_ctx:n_ctx + 3 * Q_BLOCK], vb))
    y_lat = from_heads(o.reshape(b, hk * g, t, d))
    if need_ctx:
        s = jnp.einsum('bhgqd,bhcd->bhgqc', qc, kc).astype(jnp.float32) * scale
        s_sink_c = jnp.broadcast_to(sink_f[None, :, :, None, None], s.shape[:-1] + (1,))
        pc = jax.nn.softmax(jnp.concatenate([s, s_sink_c], axis=-1), axis=-1)[..., :-1].astype(vc.dtype)
        oc = jnp.einsum('bhgqc,bhcd->bhgqd', pc, vc)
        y_ctx = from_heads(oc.reshape(b, hk * g, n_ctx, d))
    else:
        y_ctx = None
    return y_lat, y_ctx

def gla_chunk_scan(q, k, v, log_a, s0, with_out):
    b, h, t, dk = q.shape
    dv = v.shape[-1]
    n = t // C_CHUNK

    def chunks(z):
        return z.astype(jnp.float32).reshape(b, h, n, C_CHUNK, z.shape[-1]).transpose(2, 0, 1, 3, 4)

    lower_tri = jnp.tril(jnp.ones((C_CHUNK, C_CHUNK), dtype=bool))[:, :, None]

    def body(state, inp):
        qi, ki, vi, lai = inp
        cum = jnp.cumsum(lai, axis=2)
        last = cum[:, :, -1:, :]
        new_state = (jnp.exp(last[:, :, 0, :])[..., None] * state
                     + jnp.einsum('bhsd,bhse->bhde', ki * jnp.exp(last - cum), vi))
        if not with_out:
            return new_state, None
        o_inter = jnp.einsum('bhtd,bhde->bhte', qi * jnp.exp(cum), state)
        diff = cum[:, :, :, None, :] - cum[:, :, None, :, :]
        decay = jnp.exp(jnp.where(lower_tri, diff, -jnp.inf))
        scores = jnp.einsum('bhtd,bhsd,bhtsd->bhts', qi, ki, decay)
        return new_state, o_inter + jnp.einsum('bhts,bhse->bhte', scores, vi)

    state, o = lax.scan(body, s0, (chunks(q), chunks(k), chunks(v), chunks(log_a)))
    if with_out:
        o = o.transpose(1, 2, 0, 3, 4).reshape(b, h, t, dv)
    return state, o

def gla_mixer(p_lat, p_ctx, w_decay, b_decay, norm_w, need_ctx):
    def project(p):
        q, k, v, r, lr_f, lr_b = split_cols(
            p, [C_HEADS * C_DK, C_HEADS * C_DK, C_HEADS * C_DV, C_HEADS * C_DV, C_DECAY_RANK, C_DECAY_RANK])
        la_f = to_heads(jax.nn.log_sigmoid((lr_f @ w_decay[0] + b_decay[0]).astype(jnp.float32)) / C_DECAY_TEMP,
                        C_HEADS, C_DK)
        la_b = to_heads(jax.nn.log_sigmoid((lr_b @ w_decay[1] + b_decay[1]).astype(jnp.float32)) / C_DECAY_TEMP,
                        C_HEADS, C_DK)
        return (to_heads(q, C_HEADS, C_DK) * C_DK ** -0.5, to_heads(k, C_HEADS, C_DK),
                to_heads(v, C_HEADS, C_DV), r, la_f, la_b)

    q, k, v, r, la_f, la_b = project(p_lat)
    qc, kc, vc, rc, lac_f, lac_b = project(p_ctx)

    def flip(z):
        return z[:, :, ::-1]

    s0 = jnp.zeros((q.shape[0], C_HEADS, C_DK, C_DV), jnp.float32)
    s_cf, o_cf = gla_chunk_scan(qc, kc, vc, lac_f, s0, need_ctx)
    s_cb, o_cb = gla_chunk_scan(flip(qc), flip(kc), flip(vc), flip(lac_b), s0, need_ctx)
    _, o_f = gla_chunk_scan(q, k, v, la_f, s_cf, True)
    _, o_b = gla_chunk_scan(flip(q), flip(k), flip(v), flip(la_b), s_cb, True)

    def readout(o, gate):
        return from_heads(rmsnorm(o.astype(gate.dtype), norm_w)) * jax.nn.silu(gate)

    y_lat = readout(o_f + flip(o_b), r)
    y_ctx = readout(o_cf + flip(o_cb), rc) if need_ctx else None
    return y_lat, y_ctx

def qknorm_gqa_mixer(p_lat, p_ctx, q_norm_w, k_norm_w, rows, cols, need_ctx):
    g = D_HEADS // D_KV_HEADS
    scale = D_HD ** -0.5

    def project(p, rope):
        q, k, v = split_cols(p, [D_HEADS * D_HD, D_KV_HEADS * D_HD, D_KV_HEADS * D_HD])
        q = rmsnorm(to_heads(q, D_HEADS, D_HD), q_norm_w)
        k = rmsnorm(to_heads(k, D_KV_HEADS, D_HD), k_norm_w)
        v = to_heads(v, D_KV_HEADS, D_HD)
        if rope:
            q, k = rope_2d(q, rows, cols), rope_2d(k, rows, cols)
        b, _, l, _ = q.shape
        return q.reshape(b, D_KV_HEADS, g, l, D_HD), k, v

    q, k, v = project(p_lat, True)
    qc, kc, vc = project(p_ctx, False)
    b, _, _, t, _ = q.shape
    y = dense_block_attention(q, jnp.concatenate([kc, k], axis=2), jnp.concatenate([vc, v], axis=2), scale)
    y_lat = from_heads(y.reshape(b, D_HEADS, t, D_HD))
    if need_ctx:
        yc = dense_block_attention(qc, kc, vc, scale)
        y_ctx = from_heads(yc.reshape(b, D_HEADS, kc.shape[2], D_HD))
    else:
        y_ctx = None
    return y_lat, y_ctx

def gated_merge(ys, gate_logits, w_branch, w_o):
    b, l, _ = gate_logits.shape
    gates = jax.nn.sigmoid(gate_logits).reshape(b, l, N_BRANCH, D_MODEL)
    z = jnp.einsum('blnw,nwd->blnd', jnp.stack(ys, axis=2), w_branch)
    return jnp.einsum('blnd,blnd->bld', gates, z) @ w_o

def sqrelu_mlp(h, w1, w2):
    return jnp.square(jax.nn.relu(h @ w1)) @ w2

def setup_inputs(seed: int = 0) -> dict:
    key = jax.random.key(seed)
    ks = jax.random.split(key, 24)
    f32 = jnp.float32
    L, D = DEPTH, D_MODEL

    def nrm(k, shape, scale):
        return jax.random.normal(k, shape, f32) * scale

    def gain(k, shape):
        return 1.0 + 0.05 * jax.random.normal(k, shape, f32)

    return {
        'x': nrm(ks[0], (BATCH, SEQ, D), 1.0),
        'c': nrm(ks[1], (BATCH, D), 1.0),
        'ctx': nrm(ks[2], (BATCH, CTX_LEN, D), 1.0),
        'c_ctx': nrm(ks[3], (D,), 1.0),
        'ada_w': nrm(ks[4], (L, D, 6 * D), 0.5 * D ** -0.5),
        'ada_b': nrm(ks[5], (L, 6 * D), 0.01),
        'norm1_w': gain(ks[6], (L, D)),
        'norm2_w': gain(ks[7], (L, D)),
        'w_in': nrm(ks[8], (L, D, IN_COLS), D ** -0.5),
        'mla_q_norm_w': gain(ks[9], (L, A_Q_RANK)),
        'mla_w_uq': nrm(ks[10], (L, A_Q_RANK, A_HEADS * (A_NOPE + A_ROPE)), A_Q_RANK ** -0.5),
        'mla_kv_norm_w': gain(ks[11], (L, A_KV_RANK)),
        'mla_w_ukv': nrm(ks[12], (L, A_KV_RANK, A_HEADS * (A_NOPE + A_V)), A_KV_RANK ** -0.5),
        'swa_sink': nrm(ks[13], (L, B_HEADS), 1.0),
        'gla_w_decay': nrm(ks[14], (L, 2, C_DECAY_RANK, C_HEADS * C_DK), C_DECAY_RANK ** -0.5),
        'gla_b_decay': nrm(ks[15], (L, 2, C_HEADS * C_DK), 0.01),
        'gla_norm_w': gain(ks[16], (L, C_DV)),
        'gqa_q_norm_w': gain(ks[17], (L, D_HD)),
        'gqa_k_norm_w': gain(ks[18], (L, D_HD)),
        'w_branch': nrm(ks[19], (L, N_BRANCH, BRANCH_W, D), BRANCH_W ** -0.5),
        'w_o': nrm(ks[20], (L, D, D), D ** -0.5),
        'mlp_w1': nrm(ks[21], (L, D, D_FF), D ** -0.5),
        'mlp_w2': nrm(ks[22], (L, D_FF, D), D_FF ** -0.5),
        'final_norm_w': gain(ks[23], (D,)),
    }

def reference(x, c, ctx, c_ctx, ada_w, ada_b, norm1_w, norm2_w, w_in,
              mla_q_norm_w, mla_w_uq, mla_kv_norm_w, mla_w_ukv, swa_sink,
              gla_w_decay, gla_b_decay, gla_norm_w, gqa_q_norm_w, gqa_k_norm_w,
              w_branch, w_o, mlp_w1, mlp_w2, final_norm_w):
    t = x.shape[1]
    ROWS = t // GRID_W
    rows = jnp.repeat(jnp.arange(ROWS), GRID_W)
    cols = jnp.tile(jnp.arange(GRID_W), ROWS)
    xc = ctx
    sc = jax.nn.silu(c)
    scc = jax.nn.silu(c_ctx)
    for l in range(DEPTH):
        need_ctx = l < DEPTH - 1
        mod = jnp.split((sc @ ada_w[l] + ada_b[l])[:, None, :], 6, axis=-1)
        mod_c = jnp.split(scc @ ada_w[l] + ada_b[l], 6, axis=-1)
        h = modulate(rmsnorm(x, norm1_w[l]), mod[0], mod[1])
        hc = modulate(rmsnorm(xc, norm1_w[l]), mod_c[0], mod_c[1])
        p = split_cols(h @ w_in[l], IN_SPLITS)
        pc = split_cols(hc @ w_in[l], IN_SPLITS)
        ya, yca = mla_mixer(p[0], pc[0], mla_q_norm_w[l], mla_w_uq[l], mla_kv_norm_w[l], mla_w_ukv[l],
                            rows, cols, need_ctx)
        yb, ycb = window_sink_mixer(p[1], pc[1], swa_sink[l], rows, cols, need_ctx)
        yg, ycg = gla_mixer(p[2], pc[2], gla_w_decay[l], gla_b_decay[l], gla_norm_w[l], need_ctx)
        yd, ycd = qknorm_gqa_mixer(p[3], pc[3], gqa_q_norm_w[l], gqa_k_norm_w[l], rows, cols, need_ctx)
        x = x + mod[2] * gated_merge([ya, yb, yg, yd], p[4], w_branch[l], w_o[l])
        x = x + mod[5] * sqrelu_mlp(modulate(rmsnorm(x, norm2_w[l]), mod[3], mod[4]), mlp_w1[l], mlp_w2[l])
        if need_ctx:
            xc = xc + mod_c[2] * gated_merge([yca, ycb, ycg, ycd], pc[4], w_branch[l], w_o[l])
            xc = xc + mod_c[5] * sqrelu_mlp(modulate(rmsnorm(xc, norm2_w[l]), mod_c[3], mod_c[4]),
                                            mlp_w1[l], mlp_w2[l])
    return rmsnorm(x, final_norm_w)


_drawn_inputs = setup_inputs


def setup_inputs(seed=0):
    import zlib

    import numpy as np

    out = dict(_drawn_inputs(seed))
    spreads = {}
    factors = {'norm1_w': 3.5,
     'mla_q_norm_w': 8.0,
     'mla_kv_norm_w': 8.0,
     'swa_sink': 64.0,
     'gla_b_decay': 8.0,
     'gla_norm_w': 7.152,
     'gqa_q_norm_w': 8.0,
     'gqa_k_norm_w': 8.0}
    for name, (base, spread) in spreads.items():
        noise = np.random.default_rng([zlib.crc32(name.encode()), seed]).standard_normal(out[name].shape)
        drawn = base * np.exp(spread * noise) if base else spread * noise
        out[name] = __import__('jax').numpy.asarray(drawn.astype(out[name].dtype))
    for name, factor in factors.items():
        out[name] = (out[name] * factor).astype(out[name].dtype)
    return out
```

```python
import numpy as np
import concourse.bass as bass
from concourse import mybir
from contextlib import ExitStack, contextmanager

P = 128
D_MODEL, SEQ, CTX, DEPTH, GRID_W = 1024, 512, 256, 2, 64
T = SEQ + CTX
KT = D_MODEL // P
NB, LB = T // P, SEQ // P
EPS, ROPE_BASE, NEG_INF = 1e-6, 10000.0, -1e30
A_HEADS, A_NOPE, A_ROPE, A_V, A_Q_RANK, A_KV_RANK = 4, 128, 64, 128, 256, 128
B_HEADS, B_KV, B_HD, WINDOW = 8, 2, 64, 128
B_GROUP = B_HEADS // B_KV
C_HEADS, C_DK, C_DV, C_RANK, C_TEMP = 4, 64, 128, 16, 16.0
D_HEADS, D_KV, D_HD = 4, 2, 128
N_BRANCH, BRANCH_W, D_FF = 4, 512, 4096
BK = BRANCH_W // P
FF_GROUPS = D_FF // D_MODEL
LEVELS = (64, 32, 16, 8, 4, 2, 1)

A0 = 0
B0 = A0 + A_Q_RANK + A_KV_RANK + A_ROPE
C_Q = B0 + (B_HEADS + 2 * B_KV) * B_HD
C_K = C_Q + C_HEADS * C_DK
C_V = C_K + C_HEADS * C_DK
C_R = C_V + C_HEADS * C_DV
C_LR = C_R + C_HEADS * C_DV
D0 = C_LR + 2 * C_RANK
G0 = D0 + (D_HEADS + 2 * D_KV) * D_HD

BRANCHES = "CABD"
BRANCH_INDEX = {"A": 0, "B": 1, "C": 2, "D": 3}
ADA_TILES = 6 * D_MODEL // P
ADA_FIRST = 2 * KT
ADA_PER_GROUP = ADA_FIRST // (D_FF // D_MODEL)
WIDE = KT + BK
MOD_SHIFT1, MOD_SCALE1, MOD_GATE1, MOD_SHIFT2, MOD_SCALE2, MOD_GATE2 = (KT * n for n in range(6))

COL, N_COLS = {}, 0
for _name, _n in (("ada_b", ADA_TILES), ("norm1", KT), ("norm2", KT), ("final", KT), ("a_q", 2), ("a_kv", 1),
                  ("c_norm", 1), ("d_q", 1), ("d_k", 1), ("c_bias", C_HEADS), ("sink", B_HEADS)):
    COL[_name] = N_COLS
    N_COLS += _n


class Signal:

    def __init__(self, sem, unit=1, half=False, credit=0):
        self.sem, self.unit, self.half, self.credit = sem, unit, half, credit


class Counts:

    def __init__(self, eng):
        self.eng, self.turn, self.jobs, self.rates, self.taken, self.body = eng, None, 0, {}, {}, {}

    def per_turn(self, sig):
        return self.rates.get(sig, self.jobs // 2 if sig.half else self.jobs)

    def next(self, sig, n=1):
        if self.turn is None:
            self.taken[sig] = self.taken.get(sig, 0) + n
            return self.taken[sig] * sig.unit + sig.credit
        self.body[sig] = self.body.get(sig, 0) + n
        first = (self.taken.get(sig, 0) + self.body[sig]) * sig.unit + sig.credit
        return self.turn * (self.per_turn(sig) * sig.unit) + first

    def job_before_last(self, sig):
        done = self.taken.get((sig, "free"), 0)
        if self.turn is None:
            self.taken[sig, "free"] = done + 1
            return done - 1 + sig.credit
        n = self.body.get((sig, "free"), 0)
        self.body[sig, "free"] = n + 1
        return self.turn * self.jobs + (done + n - 1 + sig.credit)

    @contextmanager
    def loop(self, turns, jobs, rates={}):
        with self.eng.Fori(0, turns) as turn:
            self.turn, self.jobs, self.rates = turn, jobs, rates
            yield turn
        for key, n in self.body.items():
            sig = key[0] if isinstance(key, tuple) else key
            assert n == self.per_turn(sig), (n, self.per_turn(sig))
            self.taken[key] = self.taken.get(key, 0) + n * turns
        self.turn, self.body = None, {}


class Slots:

    def __init__(self, untouched):
        self.declared, self.held, self.untouched = {}, {}, (untouched.sem, 1)

    def last(self, slot):
        return self.held.get(slot, self.untouched)

    def next(self, slot, sig):
        free = self.last(slot)
        self.declared[sig] = self.declared.get(sig, 0) + 1
        self.held[slot] = (sig.sem, self.declared[sig] + sig.credit)
        return free

    def job_before_last(self, counts, x, sig):
        before = self.declared.get(sig, 0) + sig.credit - 1 + x
        return counts.turn * counts.jobs + before

    def after_loop(self, sig, n, last_two):
        self.declared[sig] = self.declared.get(sig, 0) + n
        for k, slot in enumerate(last_two):
            self.held[slot] = (sig.sem, self.declared[sig] + sig.credit - 1 + k)


def build(nc, w_ada, w8, w12, xT, cvec, cols_d, small_d, wdec_d, tabs_d, const_d, glamask_d, winmask_d, out):
    f32, f32r, i32 = mybir.dt.float32, mybir.dt.float32r, mybir.dt.int32
    ALU, ACT, AX = mybir.AluOpType, mybir.ActivationFunctionType, mybir.AxisListType
    ctx = ExitStack()
    with ctx:
        ROW, N_ROWS = T * 4, 53
        n_const = 2 * P + (2 * SEQ + P) + len(LEVELS) * P + 2 * P + 2 * ADA_TILES + 8 * KT + 2 * N_COLS + 200
        arena_bytes = N_ROWS * ROW + 6 * WIDE * P * 4 + n_const * 4
        ctx.enter_context(nc.sbuf_tensor("arena", [P, arena_bytes // 4], f32))
        arena_at = nc.sbuf_base - arena_bytes

        def at(name, shape, dt, offset):
            return nc.alloc_sbuf_tensor_at(name, [P] + shape, dt, offset=arena_at + offset)

        def rows(name, first, n, dt=f32):
            return at(name, [n, T], dt, first * ROW)

        R_X, R_H, R_M, R_Y, R_S = 0, KT, 3 * KT, 4 * KT, 5 * KT
        X = rows("X", R_X, KT)
        Hh, Hl = rows("Hh", R_H, KT, f32r), rows("Hl", R_H + KT, KT, f32r)
        Mh, Ml = rows("Mh", R_H, KT, f32r), rows("Ml", R_H + KT, KT, f32r)
        M = rows("M", R_M, KT)
        Yh, Yl = rows("Yh", R_Y, BK, f32r), rows("Yl", R_Y + BK, BK, f32r)
        Uh, Ul = rows("Uh", R_M, KT, f32r), rows("Ul", R_M + KT, KT, f32r)
        tmp = rows("tmp", R_S, 4)
        XS = rows("XS", R_X, KT)
        SS = rows("SS", R_S, N_ROWS - R_S)
        QY = rows("QY", R_Y + BK, BK)
        qq, kk = rows("qq", R_M, C_HEADS), rows("kk", R_M + C_HEADS, C_HEADS)
        misc = SS[:, 12, :]
        V = rows("V", R_X, 4)
        at_a = (R_S + 4) * ROW
        w_small = at("w_small", [(2 * 6 + 2 * A_HEADS) * P], f32, at_a)
        w_uq = w_small[:, 0:2 * 6 * P].rearrange("p (k n) -> p k n", k=2)
        w_ukv = w_small[:, 2 * 6 * P:].rearrange("p (h n) -> p h n", n=P)
        VA = rows("VA", R_S, 4)
        ada_first = [at(f"ada_first{k}", [ADA_FIRST // 2, KT, P], f32, R_H * ROW + k * (ADA_FIRST // 2) * D_MODEL * 4) for k in range(2)]
        ada_raw = [at(f"ada_raw{k}", [KT, P], f32, (R_S + 8) * ROW + k * D_MODEL * 4) for k in range(2)]
        offset = N_ROWS * ROW
        raw, wh, wl = [], [], []
        for k in range(2):
            raw.append(at(f"raw{k}", [WIDE, P], f32, offset + k * WIDE * P * 4))
            wh.append(at(f"wh{k}", [WIDE, P], f32r, offset + (2 + k) * WIDE * P * 4))
            wl.append(at(f"wl{k}", [WIDE, P], f32r, offset + (4 + k) * WIDE * P * 4))
        offset += 6 * WIDE * P * 4
        cursor = [offset]

        def const(name, shape):
            t = at(name, shape, f32, cursor[0])
            cursor[0] += (4 * int(np.prod(shape)) + 31) // 32 * 32
            assert cursor[0] <= arena_bytes
            return t

        ident, ones = const("ident", [P]), const("ones", [P])
        tab = const("tab", [2 * SEQ + P])
        glamask = const("glamask", [len(LEVELS), P])
        winmask = const("winmask", [2, P])
        mod = const("mod", [ADA_TILES, 2])
        gain1, gain2 = const("gain1", [KT, 2]), const("gain2", [KT, 2])
        cols = const("cols", [2, N_COLS])
        cv, cs = const("cv", [KT * 2]), const("cs", [KT * 2])
        epsc = const("epsc", [1])
        negmax, sums, sink_e = const("negmax", [4]), const("sums", [4]), const("sink_e", [4])
        rowmax, recip = const("rowmax", [4]), const("recip", [4])
        tot, dec = const("tot", [NB]), const("dec", [NB])
        nsink = const("nsink", [B_HEADS])
        cos_t, sin_t, rot_t = tab[:, 0:SEQ], tab[:, SEQ:2 * SEQ], tab[:, 2 * SEQ:2 * SEQ + P]

        slot = [ctx.enter_context(nc.psum_tensor(f"slot{k}", [P, 1024], f32)) for k in range(4)]
        x_kept = nc.dram_tensor("x_kept", [P, KT, T], f32, kind="Internal").ap()

        def sig(name, **kw):
            return Signal(ctx.enter_context(nc.semaphore(name)), **kw)

        raw_full = [sig(f"raw_full{k}", unit=16, half=True) for k in range(2)]
        ada_full = [sig(f"ada_full{k}", unit=16, half=True) for k in range(2)]
        ada_first_full = [sig(f"ada_first_full{k}", unit=16) for k in range(2)]
        ada_read = sig("ada_read")
        high_done, low_done = sig("high_done"), sig("low_done")
        job_done, gate_done = sig("job_done"), sig("gate_done")
        gate_read, z_read = sig("gate_read", credit=2), sig("z_read", credit=2)
        ff_read = sig("ff_read", credit=2)
        act_own, dve_own, pool_own = sig("act_own"), sig("dve_own"), sig("pool_own")
        consts_in, tab_in, small_in = sig("consts_in", unit=16), sig("tab_in", unit=16), sig("small_in", unit=16)
        x_in, x_saved, out_saved = sig("x_in", unit=16), sig("x_saved", unit=16), sig("out_saved", unit=16)
        init_done, cs_ready, silu_e = sig("init_done"), sig("cs_ready"), sig("silu_e")
        nsink_ready = sig("nsink_ready")
        mod_read, gain_ready = sig("mod_read"), sig("gain_ready")
        squared, sum_done, ln_read, rstd_ready = sig("squared"), sig("sum_done"), sig("ln_read"), sig("rstd_ready")
        scaled, h_high, h_ready, x_updated = sig("scaled"), sig("h_high"), sig("h_ready"), sig("x_updated")
        copied, r_read, tr_done = sig("copied"), sig("r_read"), sig("tr_done")
        normed, rot_done, rot_read, roped = sig("normed"), sig("rot_done"), sig("rot_read"), sig("roped")
        proj_done = sig("proj_done")
        scores_done, max_ready, exp_ready, prob_ready = sig("scores_done"), sig("max_ready"), sig("exp_ready"), sig("prob_ready")
        prob_t, pt_ready, o_done, y_high, y_low = sig("prob_t"), sig("pt_ready"), sig("o_done"), sig("y_high"), sig("y_low")
        z_done, abs_ready, la_read = sig("z_done"), sig("abs_ready"), sig("la_read")
        diff_ready, e_ready, q_ready, k_ready, zeroed = sig("diff_ready"), sig("e_ready"), sig("q_ready"), sig("k_ready"), sig("zeroed")
        lvl_done, lvl_read, acc_first = sig("lvl_done"), sig("lvl_read"), sig("acc_first")
        inter_e, inter_qk, kt_done, kt_copied, ds_done, state_ready = (sig("inter_e"), sig("inter_qk"), sig("kt_done"),
                                                                      sig("kt_copied"), sig("ds_done"), sig("state_ready"))
        oc_done, oc_read, y_full, sil_ready = sig("oc_done"), sig("oc_read"), sig("y_full"), sig("sil_ready")
        merged, m_high, m_low = sig("merged"), sig("m_high"), sig("m_low")
        relu_ready, u_high, u_low = (sig(n, half=True) for n in ("relu_ready", "u_high", "u_low"))
        out_ready = sig("out_ready")

        block = ctx.enter_context(nc.Block())

        def queries(layer):
            return T if layer < DEPTH - 1 else SEQ

        def chunks(n):
            return ((0, SEQ), (SEQ, T)) if n == T else ((0, SEQ),)

        def sides(n):
            return ((0, SEQ, 0), (SEQ, T, 1)) if n == T else ((0, SEQ, 0),)

        def col(layer, name, k=0):
            return cols[:, layer, COL[name] + k:COL[name] + k + 1]

        PROJ = {
            "C": [("r", h) for h in range(4)] + [("misc", 0), ("q", 0), ("q", 1), ("k", 0), ("k", 1)] + [("v", h) for h in range(4)],
            "A": [("cq", 0), ("cq", 1), ("ckv", 0)],
            "B": [("q", j) for j in range(4)] + [("k", 0), ("v", 0)],
            "D": [("q", j) for j in range(4)] + [("k", 0), ("k", 1), ("v", 0), ("v", 1)],
        }
        N_PROJ = {b: len(PROJ[b]) for b in BRANCHES}

        COPIES = {b: sum({"r": 0, "v": 2}.get(kind, 1) for kind, _ in PROJ[b]) for b in BRANCHES}
        COPIES["A"] += A_HEADS + A_HEADS // 2 + A_HEADS + NB
        OTHER_COPIES = sum(COPIES[b] for b in BRANCHES[1:])

        def attention_tiles(branch, layer):
            tiles = []
            nq = queries(layer) // P
            if branch == "B":
                for g in range(B_KV):
                    for n in range(nq):
                        keys = [m for m in (n - 1, n, n + 1) if 0 <= m < LB] if n < LB else []
                        for j in range(B_GROUP):
                            tiles.append(dict(last=j == B_GROUP - 1, first=j == 0, g=g, j=j, n=n, keys=keys + list(range(LB, NB)),
                                              lat=len(keys), col=j * P, width=B_GROUP * P))
            else:
                for h in range(4):
                    for blocks, keys in ((range(LB), range(NB)), (range(LB, NB), range(LB, NB))):
                        if blocks[0] >= nq:
                            continue
                        for n in blocks:
                            tiles.append(dict(last=n == blocks[-1], first=n == blocks[0], h=h, n=n, keys=list(keys),
                                              col=(n - blocks[0]) * P, width=len(blocks) * P, q0=blocks[0] * P))
            return tiles

        def outputs(branch, layer):
            return C_HEADS if branch == "C" else sum(t["last"] for t in attention_tiles(branch, layer))

        def score_span(branch, tile):
            if branch == "B":
                return SEQ - tile["lat"] * P, T
            return (0, T) if len(tile["keys"]) == NB else (SEQ, T)

        LAG = 2
        EXP_AND_LN = "natural_log_exp_and_others"
        SCALE = {"A": (A_NOPE + A_ROPE) ** -0.5, "B": B_HD ** -0.5, "D": D_HD ** -0.5}
        PB = {"A": [XS[:, k, :] for k in range(3)], "B": [SS[:, 4 + k, :] for k in range(3)], "D": [SS[:, 4 + k, :] for k in range(3)]}
        PT = {"A": at("PT_A", [NB, SEQ], f32, (R_S + 4) * ROW), "B": at("PT_B", [NB, SEQ], f32, (R_S + 7) * ROW)}
        PT["D"] = PT["B"]
        QB, KB = XS[:, 1:5, :], XS[:, 0, :]
        KD = at("KD", [2, T], f32, (R_X + 4) * ROW)
        VT = {"C": [XS[:, 4, :], XS[:, 5, :]], "B": [XS[:, 6, :], XS[:, 6, :]], "D": [XS[:, 6, :], XS[:, 7, :]]}
        VB = at("VB", [NB, P], f32, (R_X + 5) * ROW)
        la, cumx, cumy = SS[:, 0, :], SS[:, 1, :], SS[:, 2, :]
        diff, ee = [SS[:, 3, :], XS[:, 4, :]], [SS[:, 4, :], XS[:, 5, :]]
        ks, qs = [SS[:, 5, :], XS[:, 6, :]], [SS[:, 6, :], XS[:, 7, :]]
        acc, qi, ki, kit = SS[:, 7, :], SS[:, 8, :], SS[:, 9, :], SS[:, 10, :]
        state = at("state", [NB, P], f32, (R_S + 11) * ROW)

        def level_buffer(n):
            return (n + 1) % 2

        QR, KN = XS[:, 3:5, :], [XS[:, 5, :], XS[:, 6, :], XS[:, 7, :], SS[:, 8, :]]
        KR = SS[:, 11, :]
        SQ = {"A": [SS[:, 9, :], SS[:, 10, :]], "D": [SS[:, 0, :], SS[:, 1, :]]}
        RSTD = {"A": [XS[:, 5, :], XS[:, 6, :]], "D": [SS[:, 2, :], SS[:, 3, :]]}
        ROT = {"A": SS[:, 10, :], "B": SS[:, 11, :], "D": SS[:, 11, :]}

        def flat1(ap):
            return ap.rearrange("p (a t) -> p a t", a=1)

        def output_parts(branch, tile, dst):
            if branch == "B":
                g, n = tile["g"], tile["n"]
                src = slot[3][0:B_HD, 0:tile["width"]].rearrange("p (a o s) -> p o a s", o=2, s=P)
                return [(dst[odd * B_HD:(odd + 1) * B_HD, 2 * g:2 * g + 2, n * P:(n + 1) * P], src[:, odd, :, :]) for odd in range(2)]
            return [(dst[:, tile["h"], tile["q0"]:tile["q0"] + tile["width"]], slot[3][:, 0:tile["width"]])]

        SIZES = []
        for b in BRANCHES:
            SIZES += [KT] * N_PROJ[b] + [WIDE] * KT
        SIZES += [KT] * (KT + 2 * FF_GROUPS * KT)
        N_JOBS = len(SIZES)
        ADA_STEPS = list(range(0, KT, KT // ADA_PER_GROUP))

        @block.sync
        def _(sp):
            def tile(src, dst, full, p, size):
                sp.dma_start(dst[p][:, 0:size, :], src).then_inc(full[p].sem, 16)

            for k in range(2):
                sp.dma_start(ada_first[k][:, :, :, :], w_ada[k * (ADA_FIRST // 2):(k + 1) * (ADA_FIRST // 2)].rearrange("t p k n -> p t k n")).then_inc(ada_first_full[k].sem, 16)
            at8 = at12 = jobs = 0
            first = True
            for layer in range(DEPTH):
                for section in BRANCHES + "M":
                    parts = ([(w8, N_PROJ[section], KT), (w12, KT, WIDE)] if section in BRANCHES
                             else [(w8, KT + 2 * FF_GROUPS * KT, KT)])
                    for src, n, size in parts:
                        start = at8 if src is w8 else at12
                        k = 0
                        while first and k < 2:
                            tile(src[start + k], raw, raw_full, (jobs + k) % 2, size)
                            k += 1
                        first = False
                        turns = (n - k) // 2
                        if turns > 1:
                            with sp.Fori(0, turns) as turn:
                                for x in range(2):
                                    sp.wait_ge(low_done.sem, turn * 2 + (jobs + k + x - 1))
                                    tile(src[turn * 2 + (start + k + x)], raw, raw_full, (jobs + k + x) % 2, size)
                            k += 2 * turns
                        while k < n:
                            sp.wait_ge(low_done.sem, jobs + k - 1)
                            tile(src[start + k], raw, raw_full, (jobs + k) % 2, size)
                            k += 1
                        jobs += n
                        if src is w8:
                            at8 += n
                        else:
                            at12 += n
            for k in range(KT):
                sp.wait_ge(out_ready.sem, k + 1)
                sp.dma_start(out[:, k, :], M[:, k, 0:SEQ]).then_inc(out_saved.sem, 16)
            sp.wait_ge(out_saved.sem, 16 * KT)

        @block.gpsimd
        def _(pool):
            w = Counts(pool)
            ada = [ADA_FIRST]

            def modulation_tiles(n):
                with pool.Fori(0, n // 2) as turn:
                    for k in range(2):
                        pool.wait_ge(ada_read.sem, turn * 2 + (ada[0] + k - 1))
                        pool.dma_start(ada_raw[k][:, :, :], w_ada[turn * 2 + (ada[0] + k)]).then_inc(ada_full[k].sem, 16)
                ada[0] += n

            def tables(b, layer):
                if b == "C":
                    pool.dma_start(tab[64:64 + 2 * C_RANK, 0:C_HEADS * P], wdec_d[layer]).then_inc(tab_in.sem, 16)
                else:
                    pool.dma_start(tab[:, :], tabs_d[1 if b == "D" else 0]).then_inc(tab_in.sem, 16)
                if b == "A":
                    pool.dma_start(w_small[:, :], small_d[layer]).then_inc(small_in.sem, 16)

            for dst, src in ((ident[:, :], const_d[:, 0:P]), (glamask[:, :, :], glamask_d), (winmask[:, :, :], winmask_d),
                             (cols[:, :, :], cols_d), (cv[:, :], cvec)):
                pool.dma_start(dst, src).then_inc(consts_in.sem, 16)
            for layer in range(DEPTH):
                nq = queries(layer)
                if layer == 0:
                    pool.dma_start(X[:, :, :], xT).then_inc(x_in.sem, 16)
                else:
                    pool.wait_ge(ff_read.sem, w.next(ff_read, 2 * FF_GROUPS * KT))
                    pool.dma_start(x_kept, X[:, :, :]).then_inc(x_saved.sem, 16)
                    pool.wait_ge(x_saved.sem, w.next(x_saved))
                tables("C", layer)
                for b, after in zip(BRANCHES, BRANCHES[1:] + "M"):
                    if b == "C":
                        pool.wait_ge(copied.sem, w.next(copied, COPIES["C"] + (OTHER_COPIES if layer else 0)))
                        for h in range(C_HEADS):
                            for n, m in enumerate(LEVELS):
                                if n >= 2:
                                    pool.wait_ge(lvl_done.sem, w.next(lvl_done))
                                elif h > 0:
                                    if n == 0:
                                        pool.wait_ge(lvl_done.sem, w.next(lvl_done, 3))
                                pool.memset(qs[level_buffer(n)][:, 0:nq], 0.0).then_inc(zeroed.sem, 1)
                                pool.wait_ge(e_ready.sem, w.next(e_ready))
                                pool.tensor_tensor(ks[level_buffer(n)][:, 0:nq], kk[:, h, 0:nq], ee[level_buffer(n)][:, 0:nq], ALU.mult).then_inc(k_ready.sem, 1)
                        pool.wait_ge(lvl_done.sem, w.next(lvl_done, 3))
                    pool.wait_ge(y_low.sem, w.next(y_low, outputs(b, layer)))
                    if after != "M":
                        tables(after, layer)
                    else:
                        pool.dma_start(X[:, :, :], xT if layer == 0 else x_kept).then_inc(x_in.sem, 16)
                    modulation_tiles(KT)
                if layer < DEPTH - 1:
                    modulation_tiles(ADA_FIRST)

        @block.tensor
        def _(pe):
            w, slots = Counts(pe), Slots(init_done)
            jobs = [0]

            def mm(dst, lhsT, rhs, start=True, stop=True):
                return pe.matmul(dst, lhsT, rhs, start=start, stop=stop)

            def split_product(dst, w_high, w_low, x_high, x_low, n, kts, per_k=None, w_at=0):
                for k in range(kts):
                    if per_k is not None:
                        pe.wait_ge(per_k.sem, w.next(per_k))
                    for a, (wp, xp) in enumerate(((w_high, x_high), (w_high, x_low), (w_low, x_high))):
                        for lo, hi in chunks(n):
                            last = mm(dst[:, lo:hi], wp[:, w_at + k, :], xp[:, k, lo:hi],
                                      start=k == 0 and a == 0, stop=k == kts - 1 and a == 2)
                return last

            def job(x_high, x_low, n, release, per_k=None, x=None, modulate=None):
                p = jobs[0] % 2
                pe.wait_ge(low_done.sem, w.next(low_done))
                if x is None:
                    pe.wait_ge(*slots.next(2 * p, release))
                else:
                    pe.wait_ge(release.sem, slots.job_before_last(w, x, release))
                if modulate is not None:
                    modulation_in(2 * p, modulate)
                split_product(slot[2 * p], wh[p], wl[p], x_high, x_low, n, KT, per_k).then_inc(job_done.sem, 1)
                jobs[0] += 1

            def modulation(dst, tile):
                for k in range(KT):
                    last = mm(dst, tile[:, k, :], cs[:, 2 * k:2 * k + 2], start=k == 0, stop=k == KT - 1)
                last.then_inc(ada_read.sem, 1)

            def first_modulation():
                pe.wait_ge(*slots.next(3, mod_read))
                for n in range(ADA_FIRST):
                    k, t = divmod(n, ADA_FIRST // 2)
                    if t == 0:
                        pe.wait_ge(ada_first_full[k].sem, w.next(ada_first_full[k]))
                    modulation(slot[3][:, 2 * n:2 * n + 2], ada_first[k][:, t, :, :])

            def modulation_in(where, k):
                pe.wait_ge(ada_full[k].sem, w.next(ada_full[k]))
                modulation(slot[where][:, T:T + 2], ada_raw[k])

            def ones_sum(where, src, n, release, first=True, last=True):
                if first:
                    pe.wait_ge(*slots.next(where, release))
                for lo, hi in chunks(n):
                    ins = mm(slot[where][:, lo:hi], ones[:, :], src[:, lo:hi], start=first, stop=last)
                return ins

            def norm(n):
                for k in range(KT):
                    pe.wait_ge(squared.sem, w.next(squared))
                    ones_sum(0, tmp[:, k % 2, :], n, ln_read, k == 0, k == KT - 1).then_inc(sum_done.sem, 1)

            def transposes(where, src, blocks, release):
                pe.wait_ge(*slots.next(where, release))
                for n in range(blocks):
                    last = pe.transpose(slot[where][:, n * P:(n + 1) * P], src[:, n * P:(n + 1) * P], ident[:, :])
                return last

            def rotate(where, src, parts=P):
                pe.wait_ge(*slots.next(where, rot_read))
                mm(slot[where][0:parts, 0:SEQ], rot_t[0:parts, 0:parts], src[0:parts, 0:SEQ]).then_inc(rot_done.sem, 1)

            def project(branch, nq):
                plan = PROJ[branch]
                for n in range(len(plan) + 1):
                    if n < len(plan):
                        kind = plan[n][0]
                        narrow = kind in ("r", "q", "cq")
                        job(Hh, Hl, nq if narrow else T, r_read if kind == "r" else copied, per_k=h_ready if branch == "C" and n == 0 else None)
                    if n == 0:
                        continue
                    kind, j = plan[n - 1]
                    beside = 1 + 2 * ((n - 1) % 2)
                    if kind == "v":
                        pe.wait_ge(copied.sem, slots.declared[copied] - (n < len(plan)))
                        transposes(beside, VT[branch][j % 2], NB, copied).then_inc(tr_done.sem, 1)
                    elif branch == "D":
                        pe.wait_ge(squared.sem, w.next(squared))
                        ones_sum(beside, SQ["D"][(n - 1) % 2], nq if kind == "q" else T, ln_read).then_inc(sum_done.sem, 1)
                    elif branch == "A":
                        pe.wait_ge(squared.sem, w.next(squared))
                        if kind == "cq":
                            ones_sum(1, SQ["A"][j], nq, ln_read, j == 0, j == 1).then_inc(sum_done.sem, 1)
                        else:
                            ones_sum(3, SQ["A"][0], T, ln_read).then_inc(sum_done.sem, 1)

            def branch_c(nq):
                nc_q = nq // P
                pe.wait_ge(copied.sem, w.next(copied, COPIES["C"]))
                pe.wait_ge(tab_in.sem, w.next(tab_in))

                def output(h):
                    pe.wait_ge(state_ready.sem, w.next(state_ready))
                    pe.wait_ge(lvl_read.sem, w.next(lvl_read, len(LEVELS)))
                    pe.wait_ge(*slots.next(1, oc_read))
                    for c in range(nc_q):
                        s = slice(c * P, (c + 1) * P)
                        mm(slot[1][:, s], state[:, c, :], qi[:, s], start=True, stop=False)
                        last = mm(slot[1][:, s], V[:, h, s], acc[:, s], start=False, stop=True)
                    last.then_inc(oc_done.sem, 1)
                    pe.wait_ge(squared.sem, w.next(squared))
                    ones_sum(0, kit, nq, ln_read).then_inc(sum_done.sem, 1)

                for h in range(C_HEADS):
                    pe.wait_ge(*slots.next(0, la_read))
                    for lo, hi in chunks(T):
                        last = mm(slot[0][:, lo:hi], tab[64:64 + 2 * C_RANK, h * P:(h + 1) * P], misc[64:64 + 2 * C_RANK, lo:hi])
                    last.then_inc(z_done.sem, 1)
                    if h > 0:
                        output(h - 1)
                    pe.wait_ge(inter_qk.sem, w.next(inter_qk))
                    transposes(0, ki, NB, kt_copied).then_inc(kt_done.sem, 1)
                    for n in range(len(LEVELS) + 1):
                        where = 2 + n % 2
                        pe.wait_ge(*slots.next(where, acc_first if n == 0 else lvl_read))
                        if n < len(LEVELS):
                            pe.wait_ge(k_ready.sem, w.next(k_ready))
                            pe.wait_ge(q_ready.sem, w.next(q_ready))
                            left, right = ks[level_buffer(n)], qs[level_buffer(n)]
                        else:
                            left, right = kk[:, h, :], qq[:, h, :]
                        for c in range(nc_q):
                            s = slice(c * P, (c + 1) * P)
                            last = mm(slot[where][:, s], left[:, s], right[:, s])
                        last.then_inc(lvl_done.sem, 1)
                        if n == 0:
                            pe.wait_ge(kt_copied.sem, w.next(kt_copied))
                            pe.wait_ge(*slots.next(1, state_ready))
                            for c in range(NB):
                                s = slice(c * P, (c + 1) * P)
                                last = mm(slot[1][:, s], kit[:, s], V[:, h, s])
                            last.then_inc(ds_done.sem, 1)
                output(C_HEADS - 1)
                slots.declared[y_low] = slots.declared.get(y_low, 0) + C_HEADS

            def branch_a(nq):
                pe.wait_ge(small_in.sem, w.next(small_in))
                pe.wait_ge(tab_in.sem, w.next(tab_in))
                rotate(1, misc, A_ROPE)
                pe.wait_ge(normed.sem, w.next(normed, 2))
                order = [(None, h) for h in range(A_HEADS)] + [("rope", j) for j in range(2)]
                for n, (kind, h) in enumerate(order):
                    where = 2 * (n % 2)
                    pe.wait_ge(*slots.next(where, copied))
                    block_at = h if kind is None else A_HEADS + h
                    for k in range(2):
                        for lo, hi in chunks(nq):
                            last = mm(slot[where][:, lo:hi], w_uq[:, k, block_at * P:(block_at + 1) * P], XS[:, k, lo:hi],
                                      start=k == 0, stop=k == 1)
                    last.then_inc(proj_done.sem, 1)
                pe.wait_ge(normed.sem, w.next(normed))
                for h in range(A_HEADS):
                    where = 2 * (h % 2)
                    pe.wait_ge(*slots.next(where, copied))
                    for lo, hi in chunks(T):
                        last = mm(slot[where][:, lo:hi], w_ukv[:, h, :], XS[:, 2, lo:hi])
                    last.then_inc(proj_done.sem, 1)
                for n in range(NB):
                    where = 2 * (n % 2)
                    pe.wait_ge(*slots.next(where, copied))
                    mm(slot[where][:, 0:A_HEADS * A_V], XS[:, 2, n * P:(n + 1) * P],
                       w_ukv[:, A_HEADS:2 * A_HEADS, :]).then_inc(proj_done.sem, 1)
                pe.wait_ge(copied.sem, w.next(copied, COPIES["A"]))
                for j in range(2):
                    rotate(1 + 2 * j, QR[:, j, :])
                pe.wait_ge(roped.sem, w.next(roped, 4))

            def attention(branch, layer):
                tiles = attention_tiles(branch, layer)
                values_in = 0
                for i in range(len(tiles) + LAG + 1):
                    if i < len(tiles):
                        tile = tiles[i]
                        out_s = slot[i % 2]
                        pe.wait_ge(*slots.next(i % 2, exp_ready))
                        a, b = score_span(branch, tile)
                        n = tile["n"]
                        qs_ = slice(n * P, (n + 1) * P)
                        if branch == "B":
                            g, j = tile["g"], tile["j"]
                            part = slice(g * B_HD, (g + 1) * B_HD)
                            q = QB[part, j, qs_]
                            for x, m in enumerate(tile["keys"][:tile["lat"]]):
                                dst = out_s[:, a + x * P:a + (x + 1) * P]
                                edge = m != n
                                mm(dst, q, KB[part, m * P:(m + 1) * P], start=True, stop=not edge)
                                if edge:
                                    mm(dst, ident[:, :], winmask[:, 0 if m < n else 1, :], start=False, stop=True)
                            last = mm(out_s[:, SEQ:T], q, KB[part, SEQ:T])
                        else:
                            h = tile["h"]
                            for lo, hi in ((0, SEQ), (SEQ, T)):
                                if hi <= a:
                                    continue
                                if branch == "A":
                                    part = slice((h % 2) * A_ROPE, (h % 2 + 1) * A_ROPE)
                                    mm(out_s[:, lo:hi], QY[:, h, qs_], KN[h][:, lo:hi], start=True, stop=False)
                                    last = mm(out_s[:, lo:hi], QR[part, h // 2, qs_], KR[part, lo:hi], start=False, stop=True)
                                else:
                                    last = mm(out_s[:, lo:hi], QY[:, h, qs_], KD[:, h // (D_HEADS // D_KV), lo:hi])
                        last.then_inc(scores_done.sem, 1)
                    if i > LAG and tiles[i - LAG - 1]["last"]:
                        tile = tiles[i - LAG - 1]
                        pe.wait_ge(pt_ready.sem, w.next(pt_ready, values_in))
                        values_in = 0
                        pe.wait_ge(*slots.next(3, y_low))
                        for x, m in enumerate(tile["keys"]):
                            pt = PT[branch][:, x, 0:tile["width"]]
                            flags = dict(start=x == 0, stop=x == len(tile["keys"]) - 1)
                            if branch == "B":
                                g = tile["g"]
                                last = mm(slot[3][0:B_HD, 0:tile["width"]], VB[:, m, g * B_HD:(g + 1) * B_HD], pt, **flags)
                            elif branch == "A":
                                values = VA[:, :, :].rearrange("p a t -> p (a t)")[:, m * SEQ + tile["h"] * P:m * SEQ + (tile["h"] + 1) * P]
                                last = mm(slot[3][:, 0:tile["width"]], values, pt, **flags)
                            else:
                                last = mm(slot[3][:, 0:tile["width"]], V[:, tile["h"] // 2, m * P:(m + 1) * P], pt, **flags)
                        last.then_inc(o_done.sem, 1)
                    if LAG <= i < len(tiles) + LAG:
                        tile = tiles[i - LAG]
                        pe.wait_ge(prob_ready.sem, w.next(prob_ready))
                        transposes(2, PB[branch][(i - LAG) % 3], len(tile["keys"]), pt_ready).then_inc(prob_t.sem, 1)
                        values_in += 1

            def gates(nq, groups):
                pe.wait_ge(y_low.sem, w.next(y_low, groups))
                pe.wait_ge(*slots.last(0))
                pe.wait_ge(*slots.last(1))
                pe.wait_ge(*slots.last(2))
                pe.wait_ge(*slots.last(3))

                def gate_job(x, step):
                    p = jobs[0] % 2
                    pe.wait_ge(low_done.sem, w.next(low_done))
                    if x is not None:
                        pe.wait_ge(gate_read.sem, slots.job_before_last(w, x, gate_read))
                    else:
                        pe.wait_ge(*slots.next(2 * p, gate_read))
                    split_product(slot[2 * p], wh[p], wl[p], Hh, Hl, nq, KT).then_inc(gate_done.sem, 1)
                    if x is not None:
                        pe.wait_ge(z_read.sem, slots.job_before_last(w, x, z_read))
                    else:
                        pe.wait_ge(*slots.next(2 * p + 1, z_read))
                    modulation_in(2 * p + 1, step % 2)
                    split_product(slot[2 * p + 1], wh[p], wl[p], Yh, Yl, nq, BK, w_at=KT).then_inc(job_done.sem, 1)
                    jobs[0] += 1

                turns = KT // 2 - 1
                p = jobs[0] % 2
                with w.loop(turns, 2):
                    for x in range(2):
                        gate_job(x, x)
                slots.after_loop(gate_read, 2 * turns, (2 * p, 2 * (1 - p)))
                slots.after_loop(z_read, 2 * turns, (2 * p + 1, 2 * (1 - p) + 1))
                for x in range(2):
                    gate_job(None, x)

            def mlp(nq, ada):
                pe.wait_ge(*slots.last(0))
                pe.wait_ge(*slots.last(2))

                def group(loop):
                    for x in range(KT):
                        n = ADA_STEPS.index(x) % 2 if ada and x in ADA_STEPS else None
                        job(Hh, Hl, nq, ff_read, per_k=None, x=x if loop else None, modulate=n)
                    for x in range(KT):
                        job(Uh, Ul, nq, ff_read, per_k=u_low if x == 0 else None, x=KT + x if loop else None)

                pe.wait_ge(h_ready.sem, w.next(h_ready, KT))
                p = jobs[0] % 2
                with w.loop(FF_GROUPS - 1, 2 * KT, {s: ADA_PER_GROUP // 2 for s in ada_full}):
                    group(True)
                slots.after_loop(ff_read, (FF_GROUPS - 1) * 2 * KT, (2 * p, 2 * (1 - p)))
                group(False)

            pe.wait_ge(consts_in.sem, w.next(consts_in, 5))
            pe.wait_ge(init_done.sem, w.next(init_done))
            pe.wait_ge(cs_ready.sem, w.next(cs_ready))
            for layer in range(DEPTH):
                nq = queries(layer)
                if layer == 0:
                    first_modulation()
                norm(T)
                for b in BRANCHES:
                    if b == "B":
                        pe.wait_ge(tab_in.sem, w.next(tab_in))
                    project(b, nq)
                    if b == "C":
                        branch_c(nq)
                    if b == "A":
                        branch_a(nq)
                    if b == "B":
                        pe.wait_ge(copied.sem, w.next(copied, COPIES["B"]))
                        for j in range(5):
                            rotate(1 + 2 * (j % 2), QB[:, j, :] if j < 4 else KB)
                        pe.wait_ge(roped.sem, w.next(roped, 5))
                    if b == "D":
                        pe.wait_ge(tab_in.sem, w.next(tab_in))
                        for j in range(6):
                            pe.wait_ge(normed.sem, w.next(normed))
                            rotate(1 + 2 * (j % 2), QY[:, j, :] if j < 4 else KD[:, j - 4, :])
                        pe.wait_ge(copied.sem, w.next(copied, COPIES["D"]))
                        pe.wait_ge(roped.sem, w.next(roped, 6))
                    if b != "C":
                        attention(b, layer)
                    gates(nq, outputs(b, layer))
                for k in range(KT):
                    job(Mh, Ml, nq, x_updated, per_k=m_low if k == 0 else None)
                norm(nq)
                mlp(nq, layer < DEPTH - 1)
            norm(SEQ)

        @block.scalar
        def _(act):
            w = Counts(act)
            jobs = [0]

            def done(ins):
                ins.then_inc(act_own.sem, 1)
                act.wait_ge(act_own.sem, w.next(act_own))

            def high(n, p):
                act.wait_ge(raw_full[p].sem, w.next(raw_full[p]))
                act.activation(wh[p][:, 0:SIZES[n], :], raw[p][:, 0:SIZES[n], :], ACT.Copy).then_inc(high_done.sem, 1)

            def begin_job():
                n = jobs[0] % N_JOBS
                if n + 1 < N_JOBS:
                    high(n + 1, (n + 1) % 2)
                act.wait_ge(job_done.sem, w.next(job_done))
                jobs[0] += 1
                return n % 2

            def rsqrt(where, n, dim, rstd, sums_to_take=1):
                act.wait_ge(sum_done.sem, w.next(sum_done, sums_to_take))
                act.activation(rstd[:, 0:n], slot[where][:, 0:n], ACT.Ln, scale=1.0 / dim, bias=epsc[:, 0:1]).then_inc(ln_read.sem, 1)
                act.wait_ge(ln_read.sem, w.next(ln_read))
                act.activation(rstd[:, 0:n], rstd[:, 0:n], ACT.Exp, scale=-0.5).then_inc(rstd_ready.sem, 1)

            def norm(n, gain, shift_at, from_vector):
                for k in range(KT):
                    if from_vector:
                        act.wait_ge(x_updated.sem, w.next(x_updated))
                    if k >= 2:
                        act.wait_ge(sum_done.sem, w.next(sum_done))
                    act.activation(tmp[:, k % 2, 0:n], X[:, k, 0:n], ACT.Square).then_inc(squared.sem, 1)
                rsqrt(0, n, D_MODEL, tmp[:, 2, :], 2)
                if gain is None:
                    return
                act.wait_ge(gain_ready.sem, w.next(gain_ready))
                for k in range(KT):
                    act.wait_ge(scaled.sem, w.next(scaled))
                    for lo, hi, side in sides(n):
                        done(act.activation(tmp[:, k % 2, lo:hi], tmp[:, k % 2, lo:hi], ACT.Identity,
                                            scale=gain[:, k, side:side + 1], bias=mod[:, shift_at + k, side:side + 1]))
                    act.activation(Hh[:, k, 0:n], tmp[:, k % 2, 0:n], ACT.Copy).then_inc(h_high.sem, 1)

            def project(branch, layer, nq):
                plan = PROJ[branch]

                def copy_out(n, kind, j, s):
                    nn = nq if kind in ("r", "q", "cq") else T
                    if kind == "r":
                        act.activation(QY[:, j, 0:nn], s[:, 0:nn], ACT.Sigmoid).then_inc(sil_ready.sem, 1)
                    elif kind == "misc":
                        act.activation(misc, s[:, 0:T], ACT.Copy).then_inc(copied.sem, 1)
                    elif branch == "C" and kind in "qk":
                        dst, scale = (qq, C_DK ** -0.5) if kind == "q" else (kk, 1.0)
                        for half in range(2):
                            for copy in range(2):
                                ins = act.activation(dst[copy * C_DK:(copy + 1) * C_DK, 2 * j + half, 0:nn],
                                                     s[half * C_DK:(half + 1) * C_DK, 0:nn], ACT.Copy, scale=scale)
                        ins.then_inc(copied.sem, 1)
                    elif kind == "v":
                        act.activation(VT[branch][j % 2], s[:, 0:T], ACT.Copy).then_inc(copied.sem, 1)
                    elif branch == "A":
                        if n == 2:
                            act.wait_ge(sum_done.sem, w.next(sum_done))
                        act.activation(SQ["A"][n % 2][:, 0:nn], s[:, 0:nn], ACT.Square).then_inc(squared.sem, 1)
                        act.activation(XS[:, n, 0:nn], s[:, 0:nn], ACT.Copy).then_inc(copied.sem, 1)
                    elif branch == "B":
                        act.activation(QB[:, j, 0:nn] if kind == "q" else KB[:, 0:nn], s[:, 0:nn], ACT.Copy).then_inc(copied.sem, 1)
                    else:
                        act.activation(SQ["D"][n % 2][:, 0:nn], s[:, 0:nn], ACT.Square).then_inc(squared.sem, 1)
                        act.activation(QY[:, j, 0:nn] if kind == "q" else KD[:, j, 0:nn], s[:, 0:nn], ACT.Copy).then_inc(copied.sem, 1)

                if branch == "C":
                    act.preload_act_table(ACT.Sigmoid)
                for n in range(len(plan) + 1):
                    if n < len(plan):
                        if plan[n][0] == "misc":
                            act.preload_act_table_set(EXP_AND_LN)
                        p = begin_job()
                        copy_out(n, plan[n][0], plan[n][1], slot[2 * p])
                    if n == 0:
                        continue
                    kind, j = plan[n - 1]
                    beside = 1 + 2 * ((n - 1) % 2)
                    if kind == "v":
                        act.wait_ge(tr_done.sem, w.next(tr_done))
                        dst = VB[:, :, :].rearrange("p a t -> p (a t)") if branch == "B" else V[:, j, :]
                        act.activation(dst, slot[beside][:, 0:T], ACT.Copy).then_inc(copied.sem, 1)
                    elif branch == "D":
                        if n > 2:
                            act.wait_ge(normed.sem, w.next(normed))
                        rsqrt(beside, nq if kind == "q" else T, D_HD, RSTD["D"][(n - 1) % 2])
                if branch == "A":
                    rsqrt(1, nq, A_Q_RANK, RSTD["A"][0], 1)
                    rsqrt(3, T, A_KV_RANK, RSTD["A"][1], 1)
                if branch == "D":
                    act.wait_ge(normed.sem, w.next(normed, 2))

            def branch_c(layer, nq):
                f, b = slice(0, C_DK), slice(C_DK, P)

                def norm_factors():
                    act.wait_ge(oc_done.sem, w.next(oc_done))
                    act.activation(kit[:, 0:nq], slot[1][:, 0:nq], ACT.Square).then_inc(squared.sem, 1)
                    rsqrt(0, nq, C_DV, kit)

                def output_high(h):
                    act.wait_ge(y_full.sem, w.next(y_full))
                    act.activation(Yh[:, h, 0:nq], QY[:, h, 0:nq], ACT.Copy).then_inc(y_high.sem, 1)

                def levels_over():
                    act.wait_ge(lvl_done.sem, w.next(lvl_done, len(LEVELS)))
                    act.wait_ge(q_ready.sem, w.next(q_ready, 2))
                    act.wait_ge(k_ready.sem, w.next(k_ready, 2))

                for h in range(C_HEADS):
                    bias = col(layer, "c_bias", h)
                    act.wait_ge(z_done.sem, w.next(z_done))
                    done(act.activation(diff[0][:, 0:T], slot[0][:, 0:T], ACT.Abs, bias=bias))
                    done(act.activation(diff[0][:, 0:T], diff[0][:, 0:T], ACT.Exp, scale=-1.0))
                    act.activation(diff[0][:, 0:T], diff[0][:, 0:T], ACT.Ln, bias=1.0).then_inc(abs_ready.sem, 1)
                    if h > 0:
                        norm_factors()
                        levels_over()
                    act.wait_ge(diff_ready.sem, w.next(diff_ready))
                    act.activation(ee[0][f, 0:T], cumy[f, 0:T], ACT.Exp, scale=1.0 / C_TEMP)
                    act.activation(ee[0][b, 0:T], diff[0][b, 0:T], ACT.Exp, scale=1.0 / C_TEMP)
                    act.activation(ee[1][f, 0:T], diff[0][f, 0:T], ACT.Exp, scale=1.0 / C_TEMP)
                    act.activation(ee[1][b, 0:T], cumy[b, 0:T], ACT.Exp, scale=1.0 / C_TEMP)
                    act.activation(dec[:, :], tot[:, :], ACT.Exp, scale=1.0 / C_TEMP).then_inc(inter_e.sem, 1)
                    if h > 0:
                        output_high(h - 1)
                    for n, m in enumerate(LEVELS):
                        if n == 0:
                            act.wait_ge(inter_qk.sem, w.next(inter_qk))
                        if n >= 2:
                            act.wait_ge(q_ready.sem, w.next(q_ready))
                            act.wait_ge(k_ready.sem, w.next(k_ready))
                        act.wait_ge(diff_ready.sem, w.next(diff_ready))
                        d = diff[level_buffer(n)][:, 0:nq].rearrange("p (b s) -> p b s", s=2 * m)
                        e = ee[level_buffer(n)][:, 0:nq].rearrange("p (b s) -> p b s", s=2 * m)
                        act.activation(e[:, :, 0:m], d[:, :, 0:m], ACT.Exp, scale=-1.0 / C_TEMP)
                        act.activation(e[:, :, m:2 * m], d[:, :, m:2 * m], ACT.Exp, scale=1.0 / C_TEMP).then_inc(e_ready.sem, 1)
                        if n == 0:
                            act.wait_ge(kt_done.sem, w.next(kt_done))
                            act.activation(kit, slot[0][:, 0:T], ACT.Copy).then_inc(kt_copied.sem, 1)
                        if n == 1:
                            act.wait_ge(lvl_done.sem, w.next(lvl_done))
                            act.activation(acc[:, 0:nq], slot[2][:, 0:nq], ACT.Copy).then_inc(acc_first.sem, 1)
                norm_factors()
                levels_over()
                output_high(C_HEADS - 1)

            def branch_a(nq):
                order = [("n", h) for h in range(A_HEADS)] + [("rope", j) for j in range(2)]
                for n, (kind, h) in enumerate(order):
                    act.wait_ge(proj_done.sem, w.next(proj_done))
                    act.activation(QY[:, h, 0:nq] if kind == "n" else QR[:, h, 0:nq], slot[2 * (n % 2)][:, 0:nq], ACT.Copy).then_inc(copied.sem, 1)
                act.wait_ge(normed.sem, w.next(normed, 3))
                for h in range(A_HEADS):
                    act.wait_ge(proj_done.sem, w.next(proj_done))
                    act.activation(KN[h], slot[2 * (h % 2)][:, 0:T], ACT.Copy).then_inc(copied.sem, 1)
                va = VA[:, :, :].rearrange("p a t -> p (a t)")
                for n in range(NB):
                    act.wait_ge(proj_done.sem, w.next(proj_done))
                    act.activation(va[:, n * SEQ:(n + 1) * SEQ], slot[2 * (n % 2)][:, 0:SEQ], ACT.Copy).then_inc(copied.sem, 1)

            def attention(branch, layer):
                tiles = attention_tiles(branch, layer)
                for i in range(len(tiles) + LAG + 1):
                    if i < len(tiles):
                        tile = tiles[i]
                        a, b = score_span(branch, tile)
                        s = i % 4
                        act.wait_ge(max_ready.sem, w.next(max_ready))
                        if branch == "B":
                            head = tile["g"] * B_GROUP + tile["j"]
                            act.activation(sink_e[:, s:s + 1], col(layer, "sink", head), ACT.Exp, bias=negmax[:, s:s + 1])
                        act.activation(PB[branch][i % 3][:, 0:b - a], slot[i % 2][:, a:b], ACT.Exp, bias=negmax[:, s:s + 1],
                                       scale=SCALE[branch], accum_out=sums[:, s:s + 1]).then_inc(exp_ready.sem, 1)
                    if i > LAG and tiles[i - LAG - 1]["last"]:
                        act.wait_ge(o_done.sem, w.next(o_done))
                        for hi_, ps in output_parts(branch, tiles[i - LAG - 1], Yh):
                            ins = act.activation(hi_, ps, ACT.Copy)
                        ins.then_inc(y_high.sem, 1)
                    if LAG <= i < len(tiles) + LAG:
                        tile = tiles[i - LAG]
                        n = len(tile["keys"])
                        act.wait_ge(prob_t.sem, w.next(prob_t))
                        act.activation(PT[branch][:, 0:n, tile["col"]:tile["col"] + P],
                                       slot[2][:, 0:n * P].rearrange("p (b s) -> p b s", s=P), ACT.Copy).then_inc(pt_ready.sem, 1)

            def gates(branch, nq):
                def gate_job(n, x):
                    p = (n + x) % 2
                    high_next(n, x)
                    act.wait_ge(gate_done.sem, w.next(gate_done))
                    act.wait_ge(z_read.sem, w.job_before_last(z_read))
                    act.activation(tmp[:, p, 0:nq], slot[2 * p][:, 0:nq], ACT.Sigmoid).then_inc(gate_read.sem, 1)
                    act.wait_ge(job_done.sem, w.next(job_done))

                def high_next(n, x):
                    if n + x + 1 < N_JOBS:
                        high(n + x + 1, (n + x + 1) % 2)

                n = jobs[0] % N_JOBS
                act.preload_act_table(ACT.Sigmoid)
                with w.loop(KT // 2 - 1, 2):
                    for x in range(2):
                        gate_job(n, x)
                for x in range(KT - 2, KT):
                    gate_job(n, x)
                act.preload_act_table_set(EXP_AND_LN)
                jobs[0] += KT
                if branch == "C":
                    act.wait_ge(z_read.sem, w.taken[z_read, "free"] + z_read.credit)
                else:
                    act.wait_ge(merged.sem, w.next(merged, KT))

            def mlp(nq):
                def group(n, x0, final):
                    def hidden_high(p, j):
                        act.wait_ge(ff_read.sem, w.next(ff_read))
                        act.activation(Uh[:, j, 0:nq], tmp[:, 2 + p, 0:nq], ACT.Copy).then_inc(u_high.sem, 1)

                    for x in range(2 * KT):
                        p = (n + x) % 2
                        if not (final and x == 2 * KT - 1):
                            high_at(n + x + 1)
                        if 0 < x <= KT:
                            hidden_high(1 - p, x - 1)
                        act.wait_ge(job_done.sem, w.next(job_done))
                        if x < KT:
                            act.activation(tmp[:, p, 0:nq], slot[2 * p][:, 0:nq], ACT.Relu).then_inc(relu_ready.sem, 1)
                    act.wait_ge(ff_read.sem, w.next(ff_read, KT))

                def high_at(m):
                    act.wait_ge(raw_full[m % 2].sem, w.next(raw_full[m % 2]))
                    act.activation(wh[m % 2][:, 0:KT, :], raw[m % 2][:, 0:KT, :], ACT.Copy).then_inc(high_done.sem, 1)

                n = jobs[0] % N_JOBS
                with w.loop(FF_GROUPS - 1, 2 * KT):
                    group(n, 0, False)
                group(n, 0, True)
                jobs[0] += 2 * KT * FF_GROUPS

            act.preload_act_table_set(EXP_AND_LN)
            act.wait_ge(consts_in.sem, w.next(consts_in, 5))
            act.wait_ge(init_done.sem, w.next(init_done))
            act.activation(cs[:, :], cv[:, :], ACT.Exp, scale=-1.0).then_inc(silu_e.sem, 1)
            for layer in range(DEPTH):
                nq = queries(layer)
                if layer == 0:
                    act.wait_ge(x_in.sem, w.next(x_in))
                norm(T, gain1, MOD_SHIFT1, False)
                high(0, 0)
                if layer:
                    act.wait_ge(x_saved.sem, w.next(x_saved))
                for b in BRANCHES:
                    project(b, layer, nq)
                    if b == "C":
                        branch_c(layer, nq)
                    if b == "A":
                        branch_a(nq)
                    if b != "C":
                        attention(b, layer)
                    gates(b, nq)
                for k in range(KT):
                    act.activation(Mh[:, k, 0:nq], M[:, k, 0:nq], ACT.Copy).then_inc(m_high.sem, 1)
                for k in range(KT):
                    begin_job()
                norm(nq, gain2, MOD_SHIFT2, True)
                mlp(nq)
            norm(SEQ, None, 0, False)

        @block.vector
        def _(dve):
            w = Counts(dve)
            jobs = [0]

            def done(ins):
                ins.then_inc(dve_own.sem, 1)
                dve.wait_ge(dve_own.sem, w.next(dve_own))

            def low(n, p=None):
                p = n % 2
                dve.wait_ge(high_done.sem, w.next(high_done))
                dve.tensor_tensor(wl[p][:, 0:SIZES[n], :], raw[p][:, 0:SIZES[n], :], wh[p][:, 0:SIZES[n], :].bitcast(f32),
                                  ALU.subtract).then_inc(low_done.sem, 1)

            def begin_job():
                n = jobs[0] % N_JOBS
                if n + 1 < N_JOBS:
                    low(n + 1)
                dve.wait_ge(job_done.sem, w.next(job_done))
                jobs[0] += 1
                return n % 2

            def norm(n, gain, layer):
                dve.wait_ge(rstd_ready.sem, w.next(rstd_ready))
                rstd = tmp[:, 2, 0:n]
                if gain is None:
                    for k in range(KT):
                        dve.scalar_tensor_tensor(out=M[:, k, 0:n], in0=X[:, k, 0:n], scalar=col(layer, "final", k), in1=rstd,
                                                 op0=ALU.mult, op1=ALU.mult).then_inc(out_ready.sem, 1)
                    return

                def low_part(k):
                    dve.wait_ge(h_high.sem, w.next(h_high))
                    dve.tensor_tensor(Hl[:, k, 0:n], tmp[:, k % 2, 0:n], Hh[:, k, 0:n].bitcast(f32), ALU.subtract).then_inc(h_ready.sem, 1)
                    dve.wait_ge(h_ready.sem, w.next(h_ready))

                for k in range(KT):
                    if k >= 2:
                        low_part(k - 2)
                    dve.tensor_tensor(tmp[:, k % 2, 0:n], X[:, k, 0:n], rstd, ALU.mult).then_inc(scaled.sem, 1)
                low_part(KT - 2)
                low_part(KT - 1)

            def rope(row, where, t, parts=P, src=None):
                src = row if src is None else src
                dve.wait_ge(rot_done.sem, w.next(rot_done))
                r = slice(0, parts)
                dve.tensor_tensor(t[r, 0:SEQ], slot[where][r, 0:SEQ], sin_t[r, :], ALU.mult).then_inc(rot_read.sem, 1)
                done(dve.tensor_tensor(row[r, 0:SEQ], src[r, 0:SEQ], cos_t[r, :], ALU.mult))
                dve.wait_ge(rot_read.sem, w.next(rot_read))
                dve.tensor_tensor(row[r, 0:SEQ], row[r, 0:SEQ], t[r, 0:SEQ], ALU.add).then_inc(roped.sem, 1)

            def project(branch, layer, nq):
                plan = PROJ[branch]
                for n in range(len(plan) + 1):
                    if n < len(plan):
                        p = begin_job()
                        kind, j = plan[n]
                        if kind == "r":
                            dve.wait_ge(sil_ready.sem, w.next(sil_ready))
                            dve.tensor_tensor(QY[:, j, 0:nq], slot[2 * p][:, 0:nq], QY[:, j, 0:nq], ALU.mult).then_inc(r_read.sem, 1)
                    if n > 0 and branch == "D" and plan[n - 1][0] in "qk":
                        kind, j = plan[n - 1]
                        nn = nq if kind == "q" else T
                        row = QY[:, j, 0:nn] if kind == "q" else KD[:, j, 0:nn]
                        dve.wait_ge(rstd_ready.sem, w.next(rstd_ready))
                        dve.scalar_tensor_tensor(out=row, in0=row, scalar=col(layer, "d_" + kind), in1=RSTD["D"][(n - 1) % 2][:, 0:nn],
                                                 op0=ALU.mult, op1=ALU.mult).then_inc(normed.sem, 1)

            def branch_c(layer, nq):
                f, b = slice(0, C_DK), slice(C_DK, P)
                dve.wait_ge(copied.sem, w.next(copied, COPIES["C"] + (OTHER_COPIES if layer else 0)))
                dve.wait_ge(r_read.sem, w.next(r_read, 4))

                def readout(h):
                    dve.wait_ge(oc_done.sem, w.next(oc_done))
                    dve.wait_ge(rstd_ready.sem, w.next(rstd_ready))
                    dve.tensor_tensor(kit[:, 0:nq], slot[1][:, 0:nq], kit[:, 0:nq], ALU.mult).then_inc(oc_read.sem, 1)
                    dve.wait_ge(oc_read.sem, w.next(oc_read))
                    dve.scalar_tensor_tensor(out=QY[:, h, 0:nq], in0=kit[:, 0:nq], scalar=col(layer, "c_norm"), in1=QY[:, h, 0:nq],
                                             op0=ALU.mult, op1=ALU.mult).then_inc(y_full.sem, 1)

                def output_low(h):
                    dve.wait_ge(y_full.sem, w.next(y_full))
                    dve.wait_ge(y_high.sem, w.next(y_high))
                    dve.tensor_tensor(Yl[:, h, 0:nq], QY[:, h, 0:nq], Yh[:, h, 0:nq].bitcast(f32), ALU.subtract).then_inc(y_low.sem, 1)

                for h in range(C_HEADS):
                    bias = col(layer, "c_bias", h)
                    dve.wait_ge(abs_ready.sem, w.next(abs_ready))
                    dve.tensor_scalar(la, slot[0][:, 0:T], bias, 0.0, ALU.add, ALU.min).then_inc(la_read.sem, 1)
                    dve.wait_ge(la_read.sem, w.next(la_read))
                    done(dve.tensor_tensor(la, la, diff[0], ALU.subtract))
                    cx = cumx.rearrange("p (b s) -> p b s", s=P)
                    lc = la.rearrange("p (b s) -> p b s", s=P)
                    dve.memset(cx[:, :, 0:1], 0.0)
                    for c in range(NB):
                        ins = dve.tensor_tensor_scan(cx[:, c, 1:P], ones[:, 0:P - 1], lc[:, c, 0:P - 1], 0.0, ALU.mult, ALU.add)
                    done(ins)
                    dve.tensor_tensor(cumy[f, :], cumx[f, :], la[f, :], ALU.add)
                    dve.tensor_copy(cumy[b, :], cumx[b, :])
                    done(dve.tensor_tensor(tot[:, :].unsqueeze(2), cx[:, :, P - 1:P], lc[:, :, P - 1:P], ALU.add))

                    def difference(n):
                        m = LEVELS[n]
                        blocks = nq // (2 * m)
                        mid = cumx[:, 0:nq].rearrange("p (b s) -> p b s", s=2 * m)[:, :, m:m + 1].to_broadcast([P, blocks, 2 * m])
                        dve.tensor_tensor(diff[level_buffer(n)][:, 0:nq].rearrange("p (b s) -> p b s", s=2 * m),
                                          cumy[:, 0:nq].rearrange("p (b s) -> p b s", s=2 * m), mid, ALU.subtract).then_inc(diff_ready.sem, 1)

                    def overlay(n):
                        dve.wait_ge(lvl_done.sem, w.next(lvl_done))
                        if n == 1:
                            dve.wait_ge(acc_first.sem, w.next(acc_first))
                        else:
                            dve.wait_ge(lvl_read.sem, w.next(lvl_read))
                        mask = glamask[:, n - 1:n, :].bitcast(i32).to_broadcast([P, nq // P, P])
                        dve.copy_predicated(acc[:, 0:nq].rearrange("p (b s) -> p b s", s=P), mask,
                                            slot[2 + n % 2][:, 0:nq].rearrange("p (b s) -> p b s", s=P)).then_inc(lvl_read.sem, 1)

                    totb = tot[:, :].unsqueeze(2).to_broadcast([P, NB, P])
                    dve.tensor_tensor(diff[0].rearrange("p (b s) -> p b s", s=P), totb, cumy.rearrange("p (b s) -> p b s", s=P),
                                      ALU.subtract).then_inc(diff_ready.sem, 1)
                    difference(0)
                    if h > 0:
                        readout(h - 1)
                    dve.wait_ge(inter_e.sem, w.next(inter_e))
                    dve.tensor_tensor(qi[:, 0:nq], qq[:, h, 0:nq], ee[0][:, 0:nq], ALU.mult)
                    dve.tensor_tensor(ki, kk[:, h, :], ee[1], ALU.mult).then_inc(inter_qk.sem, 1)
                    if h > 0:
                        output_low(h - 1)
                    ds = slot[1][:, 0:T].rearrange("p (b s) -> p b s", s=P)
                    orders = ((f, [LB + c for c in range(NB - LB)] + list(range(LB))),
                              (b, [NB - 1 - c for c in range(NB)]))

                    def state_step(step):
                        for part, order in orders:
                            src, dst = order[step], order[step + 1]
                            if step == 0:
                                ins = dve.tensor_copy(state[part, dst, :], ds[part, src, :])
                            else:
                                ins = dve.scalar_tensor_tensor(out=state[part, dst, :], in0=state[part, src, :], scalar=dec[part, src:src + 1],
                                                               in1=ds[part, src, :], op0=ALU.mult, op1=ALU.add)
                        return ins

                    for n, m in enumerate(LEVELS):
                        if n + 1 < len(LEVELS):
                            difference(n + 1)
                        dve.wait_ge(e_ready.sem, w.next(e_ready))
                        dve.wait_ge(zeroed.sem, w.next(zeroed))
                        q3 = qs[level_buffer(n)][:, 0:nq].rearrange("p (b s) -> p b s", s=2 * m)
                        e3 = ee[level_buffer(n)][:, 0:nq].rearrange("p (b s) -> p b s", s=2 * m)
                        s3 = qq[:, h, 0:nq].rearrange("p (b s) -> p b s", s=2 * m)
                        dve.tensor_tensor(q3[f, :, m:2 * m], s3[f, :, m:2 * m], e3[f, :, m:2 * m], ALU.mult)
                        dve.tensor_tensor(q3[b, :, 0:m], s3[b, :, 0:m], e3[b, :, 0:m], ALU.mult).then_inc(q_ready.sem, 1)
                        if n >= 2:
                            overlay(n - 1)
                        elif n == 1:
                            dve.wait_ge(lvl_done.sem, w.next(lvl_done))
                            dve.wait_ge(ds_done.sem, w.next(ds_done))
                            for part, order in orders:
                                dve.memset(state[part, order[0], :], 0.0)
                        if 1 <= n < NB - 1:
                            done(state_step(n - 1))
                        elif n == NB - 1:
                            state_step(n - 1).then_inc(state_ready.sem, 1)
                    overlay(len(LEVELS) - 1)
                    overlay(len(LEVELS))
                    dve.wait_ge(lvl_read.sem, w.next(lvl_read))
                readout(C_HEADS - 1)
                output_low(C_HEADS - 1)

            def branch_a(layer, nq):
                dve.wait_ge(rstd_ready.sem, w.next(rstd_ready))
                for k in range(2):
                    dve.scalar_tensor_tensor(out=XS[:, k, 0:nq], in0=XS[:, k, 0:nq], scalar=col(layer, "a_q", k), in1=RSTD["A"][0][:, 0:nq],
                                             op0=ALU.mult, op1=ALU.mult).then_inc(normed.sem, 1)
                dve.wait_ge(rstd_ready.sem, w.next(rstd_ready))
                dve.scalar_tensor_tensor(out=XS[:, 2, :], in0=XS[:, 2, :], scalar=col(layer, "a_kv"), in1=RSTD["A"][1],
                                         op0=ALU.mult, op1=ALU.mult).then_inc(normed.sem, 1)
                rope(KR, 1, ROT["A"], A_ROPE, src=misc)
                dve.wait_ge(roped.sem, w.next(roped))
                done(dve.tensor_copy(KR[0:A_ROPE, SEQ:T], misc[0:A_ROPE, SEQ:T]))
                dve.tensor_copy(KR[A_ROPE:P, :], KR[0:A_ROPE, :]).then_inc(roped.sem, 1)
                dve.wait_ge(roped.sem, w.next(roped))
                for j in range(2):
                    rope(QR[:, j, :], 1 + 2 * j, ROT["A"])
                    dve.wait_ge(roped.sem, w.next(roped))

            def attention(branch, layer):
                tiles = attention_tiles(branch, layer)
                for i in range(len(tiles) + LAG + 1):
                    if i < len(tiles):
                        tile = tiles[i]
                        a, b = score_span(branch, tile)
                        s = i % 4
                        dve.wait_ge(scores_done.sem, w.next(scores_done))
                        done(dve.reduce_max(rowmax[:, s:s + 1], slot[i % 2][:, a:b], axis=AX.X))
                        if branch == "B":
                            head = tile["g"] * B_GROUP + tile["j"]
                            ins = dve.tensor_scalar(negmax[:, s:s + 1], rowmax[:, s:s + 1], -SCALE[branch], nsink[:, head:head + 1], ALU.mult, ALU.min)
                        else:
                            ins = dve.tensor_scalar(negmax[:, s:s + 1], rowmax[:, s:s + 1], -SCALE[branch], None, ALU.mult)
                        ins.then_inc(max_ready.sem, 1)
                    if 1 <= i <= len(tiles):
                        tile = tiles[i - 1]
                        a, b = score_span(branch, tile)
                        s = (i - 1) % 4
                        dve.wait_ge(exp_ready.sem, w.next(exp_ready))
                        if branch == "B":
                            done(dve.tensor_tensor(sums[:, s:s + 1], sums[:, s:s + 1], sink_e[:, s:s + 1], ALU.add))
                        done(dve.reciprocal(recip[:, s:s + 1], sums[:, s:s + 1]))
                        pb = PB[branch][(i - 1) % 3][:, 0:b - a]
                        dve.tensor_scalar(pb, pb, recip[:, s:s + 1], None, ALU.mult).then_inc(prob_ready.sem, 1)
                    if i > LAG and tiles[i - LAG - 1]["last"]:
                        dve.wait_ge(y_high.sem, w.next(y_high))
                        for (lo_, ps), (hi_, _) in zip(output_parts(branch, tiles[i - LAG - 1], Yl), output_parts(branch, tiles[i - LAG - 1], Yh)):
                            ins = dve.tensor_tensor(lo_, ps, hi_.bitcast(f32), ALU.subtract)
                        ins.then_inc(y_low.sem, 1)

            def modulation_ready(layer, first, end, gain, name, scale_at):
                bias = cols[:, layer, COL["ada_b"] + first:COL["ada_b"] + end].unsqueeze(2).to_broadcast([P, end - first, 2])
                done(dve.tensor_tensor(mod[:, first:end, :], mod[:, first:end, :], bias, ALU.add))
                done(dve.tensor_scalar_add(gain[:, :, :], mod[:, scale_at:scale_at + KT, :], 1.0))
                nw = cols[:, layer, COL[name]:COL[name] + KT].unsqueeze(2).to_broadcast([P, KT, 2])
                dve.tensor_tensor(gain[:, :, :], gain[:, :, :], nw, ALU.mult).then_inc(gain_ready.sem, 1)

            def gates(branch, nq):
                n = jobs[0] % N_JOBS
                mod_at = ADA_FIRST + KT * BRANCHES.index(branch)

                def gate_job(x, row, last):
                    p = (n + x) % 2
                    if not last or n + x + 1 < N_JOBS:
                        low(n + x + 1)
                    dve.wait_ge(gate_read.sem, w.next(gate_read))
                    dve.wait_ge(job_done.sem, w.next(job_done))
                    dve.tensor_copy(mod[:, bass.ds(row + mod_at, 1), :], flat1(slot[2 * p + 1][:, T:T + 2]))
                    g, z = tmp[:, p, 0:nq], slot[2 * p + 1][:, 0:nq]
                    m = M[:, bass.ds(row, 1), 0:nq]
                    if branch == BRANCHES[0]:
                        dve.tensor_tensor(m, flat1(g), flat1(z), ALU.mult).then_inc(z_read.sem, 1)
                    else:
                        t = tmp[:, 2 + p, 0:nq]
                        dve.tensor_tensor(t, g, z, ALU.mult).then_inc(z_read.sem, 1)
                        dve.wait_ge(z_read.sem, w.next(z_read))
                        dve.tensor_tensor(m, m, flat1(t), ALU.add).then_inc(merged.sem, 1)
                        dve.wait_ge(merged.sem, w.next(merged))

                with w.loop(KT // 2 - 1, 2) as turn:
                    for x in range(2):
                        gate_job(x, turn * 2 + x, False)
                for x in range(KT - 2, KT):
                    gate_job(x, x, True)
                if branch == BRANCHES[0]:
                    dve.wait_ge(z_read.sem, w.next(z_read, KT))
                jobs[0] += KT

            def mlp(nq, ada):
                n = jobs[0] % N_JOBS

                def group(first_tile, final):
                    def hidden_low(p, j):
                        dve.wait_ge(u_high.sem, w.next(u_high))
                        dve.tensor_tensor(Ul[:, j, 0:nq], tmp[:, 2 + p, 0:nq], Uh[:, j, 0:nq].bitcast(f32), ALU.subtract).then_inc(u_low.sem, 1)
                        dve.wait_ge(u_low.sem, w.next(u_low))

                    for x in range(2 * KT):
                        p = (n + x) % 2
                        if not (final and x == 2 * KT - 1):
                            dve.wait_ge(high_done.sem, w.next(high_done))
                            q = 1 - p
                            dve.tensor_tensor(wl[q][:, 0:KT, :], raw[q][:, 0:KT, :], wh[q][:, 0:KT, :].bitcast(f32), ALU.subtract).then_inc(low_done.sem, 1)
                        if 0 < x <= KT:
                            hidden_low(1 - p, x - 1)
                        dve.wait_ge(job_done.sem, w.next(job_done))
                        if x < KT:
                            dve.wait_ge(relu_ready.sem, w.next(relu_ready))
                            if ada and x in ADA_STEPS:
                                dve.tensor_copy(mod[:, bass.ds(first_tile + ADA_STEPS.index(x), 1), :], flat1(slot[2 * p][:, T:T + 2]))
                            dve.tensor_tensor(tmp[:, 2 + p, 0:nq], slot[2 * p][:, 0:nq], tmp[:, p, 0:nq], ALU.mult).then_inc(ff_read.sem, 1)
                        if x >= KT:
                            add_to_x(x - KT, 2 * p, MOD_GATE2, nq).then_inc(ff_read.sem, 1)
                    dve.wait_ge(ff_read.sem, w.next(ff_read, 2 * KT))

                with w.loop(FF_GROUPS - 1, 2 * KT) as turn:
                    group(turn * ADA_PER_GROUP, False)
                group(ADA_PER_GROUP * (FF_GROUPS - 1), True)
                jobs[0] += 2 * KT * FF_GROUPS

            def add_to_x(k, where, gate_at, n):
                for lo, hi, side in sides(n):
                    ins = dve.scalar_tensor_tensor(out=X[:, k, lo:hi], in0=slot[where][:, lo:hi], scalar=mod[:, gate_at + k, side:side + 1],
                                                   in1=X[:, k, lo:hi], op0=ALU.mult, op1=ALU.add)
                return ins

            for n_, s_ in enumerate((gate_read, z_read, ff_read)):
                dve.memset(rowmax[:, n_:n_ + 1], 0.0).then_inc(s_.sem, s_.credit)
            dve.memset(epsc[:, :], EPS)
            dve.memset(ones[:, :], 1.0).then_inc(init_done.sem, 1)
            dve.wait_ge(consts_in.sem, w.next(consts_in, 5))
            dve.wait_ge(init_done.sem, w.next(init_done))
            dve.wait_ge(silu_e.sem, w.next(silu_e))
            done(dve.tensor_scalar_add(cs[:, :], cs[:, :], 1.0))
            done(dve.reciprocal(cs[:, :], cs[:, :]))
            dve.tensor_tensor(cs[:, :], cs[:, :], cv[:, :], ALU.mult).then_inc(cs_ready.sem, 1)
            for layer in range(DEPTH):
                nq = queries(layer)
                if layer == 0:
                    dve.wait_ge(ada_read.sem, w.next(ada_read, ADA_FIRST))
                    dve.tensor_copy(mod[:, 0:ADA_FIRST, :], slot[3][:, 0:2 * ADA_FIRST].rearrange("p (a s) -> p a s", s=2)).then_inc(mod_read.sem, 1)
                    dve.wait_ge(mod_read.sem, w.next(mod_read))
                modulation_ready(layer, 0, ADA_FIRST, gain1, "norm1", MOD_SCALE1)
                dve.tensor_scalar(nsink[:, :], cols[:, layer, COL["sink"]:COL["sink"] + B_HEADS], -1.0, None, ALU.mult).then_inc(nsink_ready.sem, 1)
                if layer == 0:
                    dve.wait_ge(x_in.sem, w.next(x_in))
                norm(T, gain1, layer)
                dve.wait_ge(nsink_ready.sem, w.next(nsink_ready))
                low(0)
                for b in BRANCHES:
                    project(b, layer, nq)
                    if b == "C":
                        branch_c(layer, nq)
                    dve.wait_ge(tab_in.sem, w.next(tab_in))
                    if b == "A":
                        branch_a(layer, nq)
                    if b == "B":
                        for j in range(5):
                            rope(QB[:, j, :] if j < 4 else KB, 1 + 2 * (j % 2), ROT["B"])
                            dve.wait_ge(roped.sem, w.next(roped))
                    if b == "D":
                        for j in range(6):
                            rope(QY[:, j, :] if j < 4 else KD[:, j - 4, :], 1 + 2 * (j % 2), ROT["D"])
                            dve.wait_ge(roped.sem, w.next(roped))
                    if b != "C":
                        attention(b, layer)
                    gates(b, nq)
                modulation_ready(layer, ADA_FIRST, ADA_TILES, gain2, "norm2", MOD_SCALE2)
                for k in range(KT):
                    dve.wait_ge(m_high.sem, w.next(m_high))
                    dve.tensor_tensor(Ml[:, k, 0:nq], M[:, k, 0:nq], Mh[:, k, 0:nq].bitcast(f32), ALU.subtract).then_inc(m_low.sem, 1)
                dve.wait_ge(x_in.sem, w.next(x_in))
                for k in range(KT):
                    p = begin_job()
                    add_to_x(k, 2 * p, MOD_GATE1, nq).then_inc(x_updated.sem, 1)
                dve.wait_ge(x_updated.sem, w.next(x_updated, KT))
                norm(nq, gain2, layer)
                mlp(nq, layer < DEPTH - 1)
            norm(SEQ, None, DEPTH - 1)


def tiles_of(w, cols):
    k = w.shape[0]
    return np.ascontiguousarray(w[:, cols].reshape(k // P, P, len(cols) // P, P).transpose(2, 1, 0, 3))


def rope_table(dim):
    half, quarter = dim // 2, dim // 4
    t = np.arange(SEQ)
    inv = (ROPE_BASE ** (-np.arange(quarter, dtype=np.float32) / quarter)).astype(np.float32)
    cos, sin, rot = np.zeros((P, SEQ), np.float32), np.zeros((P, SEQ), np.float32), np.zeros((P, P), np.float32)
    for p in range(P):
        f = p % dim
        pos = (t // GRID_W if f < half else t % GRID_W).astype(np.float32)
        ang = pos * inv[f % quarter]
        cos[p], sin[p] = np.cos(ang), np.sin(ang)
        if f % half < quarter:
            rot[p + quarter, p] = -1.0
        else:
            rot[p - quarter, p] = 1.0
    return np.concatenate([cos, sin, rot], axis=1)


def kernel(x, c, ctx, c_ctx, ada_w, ada_b, norm1_w, norm2_w, w_in, mla_q_norm_w, mla_w_uq, mla_kv_norm_w, mla_w_ukv,
           swa_sink, gla_w_decay, gla_b_decay, gla_norm_w, gqa_q_norm_w, gqa_k_norm_w, w_branch, w_o, mlp_w1, mlp_w2,
           final_norm_w):
    import concourse.bacc as bacc
    from concourse.bass_utils import run_bass_kernel_spmd

    (x, c, ctx, c_ctx, ada_w, ada_b, norm1_w, norm2_w, w_in, mla_q_norm_w, mla_w_uq, mla_kv_norm_w, mla_w_ukv, swa_sink,
     gla_w_decay, gla_b_decay, gla_norm_w, gqa_q_norm_w, gqa_k_norm_w, w_branch, w_o, mlp_w1, mlp_w2, final_norm_w) = [
        np.asarray(a) for a in (x, c, ctx, c_ctx, ada_w, ada_b, norm1_w, norm2_w, w_in, mla_q_norm_w, mla_w_uq,
                                mla_kv_norm_w, mla_w_ukv, swa_sink, gla_w_decay, gla_b_decay, gla_norm_w, gqa_q_norm_w,
                                gqa_k_norm_w, w_branch, w_o, mlp_w1, mlp_w2, final_norm_w)]
    feature_major = lambda a: np.ascontiguousarray(a.reshape(-1, KT, P).transpose(2, 1, 0))
    span = lambda start, n: np.arange(start, start + n)
    ada, w8, w12, cols, small, wdec = [], [], [], [], [], []
    for l in range(DEPTH):
        ada.append(tiles_of(ada_w[l], span(0, 6 * D_MODEL)))
        zero = np.zeros((D_MODEL, P - A_ROPE - 2 * C_RANK), np.float32)
        misc = np.concatenate([w_in[l][:, span(A0 + A_Q_RANK + A_KV_RANK, A_ROPE)], w_in[l][:, span(C_LR, 2 * C_RANK)], zero], 1)
        w8 += [tiles_of(w_in[l], span(C_R, 512)), tiles_of(misc, span(0, P)), tiles_of(w_in[l], span(C_Q, 256)),
               tiles_of(w_in[l], span(C_K, 256)), tiles_of(w_in[l], span(C_V, 512))]
        w8.append(tiles_of(w_in[l], span(A0, A_Q_RANK + A_KV_RANK)))
        heads = [g * B_GROUP + j for j in range(B_GROUP) for g in range(B_KV)]
        w8.append(tiles_of(w_in[l], np.concatenate([span(B0 + h * B_HD, B_HD) for h in heads])))
        w8.append(tiles_of(w_in[l], span(B0 + B_HEADS * B_HD, 2 * B_KV * B_HD)))
        w8.append(tiles_of(w_in[l], span(D0, (D_HEADS + 2 * D_KV) * D_HD)))
        w8.append(tiles_of(w_o[l], span(0, D_MODEL)))
        for g in range(FF_GROUPS):
            w8.append(tiles_of(mlp_w1[l], span(g * D_MODEL, D_MODEL)))
            w8.append(tiles_of(mlp_w2[l][g * D_MODEL:(g + 1) * D_MODEL], span(0, D_MODEL)))
        for b in BRANCHES:
            i = BRANCH_INDEX[b]
            gate = tiles_of(w_in[l], span(G0 + i * D_MODEL, D_MODEL))
            w12.append(np.concatenate([gate, tiles_of(w_branch[l, i], span(0, D_MODEL))], axis=2))
        per = lambda a: a.reshape(-1, P).T
        decay_bias = np.stack([np.concatenate([gla_b_decay[l, d, h * C_DK:(h + 1) * C_DK] for d in range(2)]) for h in range(C_HEADS)], 1)
        cols.append(np.concatenate([per(ada_b[l]), per(norm1_w[l]), per(norm2_w[l]), per(final_norm_w), per(mla_q_norm_w[l]),
                                    per(mla_kv_norm_w[l]), per(gla_norm_w[l]), per(gqa_q_norm_w[l]), per(gqa_k_norm_w[l]),
                                    decay_bias, np.broadcast_to(swa_sink[l], (P, B_HEADS))], axis=1))
        uq = mla_w_uq[l].reshape(2, P, A_HEADS, A_NOPE + A_ROPE)
        uq = np.concatenate([uq[..., :A_NOPE].reshape(2, P, -1), uq[..., A_NOPE:].reshape(2, P, -1)], axis=2).transpose(1, 0, 2)
        ukv = mla_w_ukv[l].reshape(P, A_HEADS, 2, P).transpose(0, 2, 1, 3)
        small.append(np.concatenate([uq.reshape(P, -1), ukv.reshape(P, -1)], axis=1))
        wd = np.zeros((2, C_RANK, C_HEADS, 2, C_DK), np.float32)
        for d in range(2):
            wd[d, :, :, d, :] = gla_w_decay[l, d].reshape(C_RANK, C_HEADS, C_DK)
        wdec.append(wd.reshape(2 * C_RANK, C_HEADS * P))
    s, t = np.arange(P)[:, None, None], np.arange(P)[None, None, :]
    halves = np.array(LEVELS[1:])[None, :, None]
    mask = (s // (2 * halves) == t // (2 * halves)) & (s // halves != t // halves)
    mask = np.concatenate([mask, s == t], axis=1).astype(np.float32)
    win = np.stack([np.where(t[:, 0] >= s[:, 0], 0.0, NEG_INF), np.where(t[:, 0] <= s[:, 0], 0.0, NEG_INF)], 1).astype(np.float32)
    arrays = {
        "ada": np.concatenate(ada),
        "w8": np.concatenate(w8), "w12": np.concatenate(w12),
        "xT": feature_major(np.concatenate([x[0], ctx[0]], axis=0)),
        "cvec": feature_major(np.stack([c[0], c_ctx])).reshape(P, 2 * KT),
        "cols": np.ascontiguousarray(np.stack(cols, axis=1)), "small": np.stack(small), "wdec": np.stack(wdec),
        "tabs": np.stack([rope_table(A_ROPE), rope_table(D_HD)]), "ident": np.eye(P, dtype=np.float32),
        "glamask": mask, "winmask": win,
    }
    nc = bacc.Bacc("TRN2", target_bir_lowering=False, num_devices=1)
    aps = [nc.dram_tensor(f"{n}_dram", a.shape, mybir.dt.from_np(a.dtype), kind="ExternalInput").ap() for n, a in arrays.items()]
    out = nc.dram_tensor("out_dram", (P, KT, SEQ), mybir.dt.float32, kind="ExternalOutput").ap()
    build(nc, *aps, out)
    r = run_bass_kernel_spmd(nc, [{f"{n}_dram": a for n, a in arrays.items()}], core_ids=[0])
    y = r.results[0]["out_dram"]
    return np.ascontiguousarray(y.transpose(2, 1, 0).reshape(1, SEQ, D_MODEL))
```

```python
import numpy as np
import concourse.bass as bass
from concourse import mybir
from contextlib import ExitStack, contextmanager

P = 128
D_MODEL, SEQ, CTX, DEPTH, GRID_W = 1024, 512, 256, 2, 64
T = SEQ + CTX
KT = D_MODEL // P
NB, LB = T // P, SEQ // P
EPS, ROPE_BASE, NEG_INF = 1e-6, 10000.0, -1e30
A_HEADS, A_NOPE, A_ROPE, A_V, A_Q_RANK, A_KV_RANK = 4, 128, 64, 128, 256, 128
B_HEADS, B_KV, B_HD, WINDOW = 8, 2, 64, 128
B_GROUP = B_HEADS // B_KV
C_HEADS, C_DK, C_DV, C_RANK, C_TEMP = 4, 64, 128, 16, 16.0
D_HEADS, D_KV, D_HD = 4, 2, 128
N_BRANCH, BRANCH_W, D_FF = 4, 512, 4096
BK = BRANCH_W // P
FF_GROUPS = D_FF // D_MODEL
LEVELS = (64, 32, 16, 8, 4, 2, 1)

A0 = 0
B0 = A0 + A_Q_RANK + A_KV_RANK + A_ROPE
C_Q = B0 + (B_HEADS + 2 * B_KV) * B_HD
C_K = C_Q + C_HEADS * C_DK
C_V = C_K + C_HEADS * C_DK
C_R = C_V + C_HEADS * C_DV
C_LR = C_R + C_HEADS * C_DV
D0 = C_LR + 2 * C_RANK
G0 = D0 + (D_HEADS + 2 * D_KV) * D_HD

BRANCHES = "CABD"
BRANCH_INDEX = {"A": 0, "B": 1, "C": 2, "D": 3}
ADA_TILES = 6 * D_MODEL // P
ADA_FIRST = 2 * KT
ADA_PER_HEAD = (ADA_TILES - ADA_FIRST) // C_HEADS
ADA_PER_GROUP = ADA_FIRST // (D_FF // D_MODEL)
WIDE = KT + BK
MOD_SHIFT1, MOD_SCALE1, MOD_GATE1, MOD_SHIFT2, MOD_SCALE2, MOD_GATE2 = (KT * n for n in range(6))

PROJ = {
    "C": [("r", h) for h in range(4)] + [("misc", 0), ("q", 0), ("q", 1), ("k", 0), ("k", 1)] + [("v", h) for h in range(4)],
    "A": [("cq", 0), ("cq", 1), ("ckv", 0)],
    "B": [("q", j) for j in range(4)] + [("k", 0), ("v", 0)],
    "D": [("q", j) for j in range(4)] + [("k", 0), ("k", 1), ("v", 0), ("v", 1)],
}
N_PROJ = {b: len(PROJ[b]) for b in BRANCHES}

COL, N_COLS = {}, 0
for _name, _n in (("ada_b", ADA_TILES), ("norm1", KT), ("norm2", KT), ("final", KT), ("a_q", 2), ("a_kv", 1),
                  ("c_norm", 1), ("d_q", 1), ("d_k", 1), ("c_bias", C_HEADS), ("sink", B_HEADS)):
    COL[_name] = N_COLS
    N_COLS += _n


class Signal:

    def __init__(self, sem, unit=1, half=False, credit=0):
        self.sem, self.unit, self.half, self.credit = sem, unit, half, credit


class Counts:

    def __init__(self, eng):
        self.eng, self.turn, self.jobs, self.rates, self.taken, self.body = eng, None, 0, {}, {}, {}

    def per_turn(self, sig):
        return self.rates.get(sig, self.jobs // 2 if sig.half else self.jobs)

    def next(self, sig, n=1):
        if self.turn is None:
            self.taken[sig] = self.taken.get(sig, 0) + n
            return self.taken[sig] * sig.unit + sig.credit
        self.body[sig] = self.body.get(sig, 0) + n
        first = (self.taken.get(sig, 0) + self.body[sig]) * sig.unit + sig.credit
        return self.turn * (self.per_turn(sig) * sig.unit) + first

    def job_before_last(self, sig):
        done = self.taken.get((sig, "free"), 0)
        if self.turn is None:
            self.taken[sig, "free"] = done + 1
            return done - 1 + sig.credit
        n = self.body.get((sig, "free"), 0)
        self.body[sig, "free"] = n + 1
        return self.turn * self.jobs + (done + n - 1 + sig.credit)

    @contextmanager
    def loop(self, turns, jobs, rates={}):
        with self.eng.Fori(0, turns) as turn:
            self.turn, self.jobs, self.rates = turn, jobs, rates
            yield turn
        for key, n in self.body.items():
            sig = key[0] if isinstance(key, tuple) else key
            assert n == self.per_turn(sig), (n, self.per_turn(sig))
            self.taken[key] = self.taken.get(key, 0) + n * turns
        self.turn, self.body = None, {}


class Slots:

    def __init__(self, untouched):
        self.declared, self.held, self.untouched = {}, {}, (untouched.sem, 1)

    def last(self, slot):
        return self.held.get(slot, self.untouched)

    def next(self, slot, sig):
        free = self.last(slot)
        self.declared[sig] = self.declared.get(sig, 0) + 1
        self.held[slot] = (sig.sem, self.declared[sig] + sig.credit)
        return free

    def job_before_last(self, counts, x, sig):
        before = self.declared.get(sig, 0) + sig.credit - 1 + x
        return counts.turn * counts.jobs + before

    def after_loop(self, sig, n, last_two):
        self.declared[sig] = self.declared.get(sig, 0) + n
        for k, slot in enumerate(last_two):
            self.held[slot] = (sig.sem, self.declared[sig] + sig.credit - 1 + k)


def build(nc, w_ada, w8, w12, xT, cvec, cols_d, small_d, wdec_d, tabs_d, const_d, glamask_d, winmask_d, out):
    f32, f32r, i32 = mybir.dt.float32, mybir.dt.float32r, mybir.dt.int32
    ALU, ACT, AX = mybir.AluOpType, mybir.ActivationFunctionType, mybir.AxisListType
    ctx = ExitStack()
    with ctx:
        ROW, N_ROWS = T * 4, 53
        n_const = 2 * P + (2 * SEQ + P) + len(LEVELS) * P + 2 * P + 2 * ADA_TILES + 8 * KT + 2 * N_COLS + 200
        arena_bytes = N_ROWS * ROW + 6 * WIDE * P * 4 + n_const * 4
        ctx.enter_context(nc.sbuf_tensor("arena", [P, arena_bytes // 4], f32))
        arena_at = nc.sbuf_base - arena_bytes

        def at(name, shape, dt, offset):
            return nc.alloc_sbuf_tensor_at(name, [P] + shape, dt, offset=arena_at + offset)

        def rows(name, first, n, dt=f32):
            return at(name, [n, T], dt, first * ROW)

        R_X, R_H, R_M, R_Y, R_S = 0, KT, 3 * KT, 4 * KT, 5 * KT
        X = rows("X", R_X, KT)
        Hh, Hl = rows("Hh", R_H, KT, f32r), rows("Hl", R_H + KT, KT, f32r)
        Mh, Ml = rows("Mh", R_H, KT, f32r), rows("Ml", R_H + KT, KT, f32r)
        M = rows("M", R_M, KT)
        Yh, Yl = rows("Yh", R_Y, BK, f32r), rows("Yl", R_Y + BK, BK, f32r)
        Uh, Ul = rows("Uh", R_M, KT, f32r), rows("Ul", R_M + KT, KT, f32r)
        tmp = rows("tmp", R_S, 4)
        XS = rows("XS", R_X, KT)
        SS = rows("SS", R_S, N_ROWS - R_S)
        QY = rows("QY", R_Y + BK, BK)
        qq, kk = rows("qq", R_M, C_HEADS), rows("kk", R_M + C_HEADS, C_HEADS)
        misc = SS[:, 12, :]
        V = rows("V", R_X, 4)
        at_a = (R_S + 4) * ROW
        w_small = at("w_small", [(2 * 6 + 2 * A_HEADS) * P], f32, at_a)
        w_uq = w_small[:, 0:2 * 6 * P].rearrange("p (k n) -> p k n", k=2)
        w_ukv = w_small[:, 2 * 6 * P:].rearrange("p (h n) -> p h n", n=P)
        VA = rows("VA", R_S, 4)
        ada_first = [at(f"ada_first{k}", [ADA_FIRST // 2, KT, P], f32, R_H * ROW + k * (ADA_FIRST // 2) * D_MODEL * 4) for k in range(2)]
        ada_raw = [at(f"ada_raw{k}", [KT, P], f32, (R_S + 8) * ROW + k * D_MODEL * 4) for k in range(2)]
        mod_first_t = at("mod_first_t", [ADA_FIRST * P], f32, (R_S + 4) * ROW)
        offset = N_ROWS * ROW
        raw, wh, wl = [], [], []
        for k in range(2):
            raw.append(at(f"raw{k}", [WIDE, P], f32, offset + k * WIDE * P * 4))
            wh.append(at(f"wh{k}", [WIDE, P], f32r, offset + (2 + 2 * k) * WIDE * P * 4))
            wl.append(at(f"wl{k}", [WIDE, P], f32r, offset + (3 + 2 * k) * WIDE * P * 4))
        free_pair = offset + (2 + 2 * ((N_PROJ["C"] - 1) % 2)) * WIDE * P * 4
        ada_c_raw = [at(f"ada_c_raw{k}", [KT, P], f32, free_pair + k * D_MODEL * 4) for k in range(2)]
        mod_c_t = at("mod_c_t", [ADA_PER_HEAD * P], f32, free_pair + 2 * D_MODEL * 4)
        offset += 6 * WIDE * P * 4
        cursor = [offset]

        def const(name, shape):
            t = at(name, shape, f32, cursor[0])
            cursor[0] += (4 * int(np.prod(shape)) + 31) // 32 * 32
            assert cursor[0] <= arena_bytes
            return t

        ident, ones = const("ident", [P]), const("ones", [P])
        tab = const("tab", [2 * SEQ + P])
        glamask = const("glamask", [len(LEVELS), P])
        winmask = const("winmask", [2, P])
        mod = const("mod", [ADA_TILES, 2])
        gain1, gain2 = const("gain1", [KT, 2]), const("gain2", [KT, 2])
        cols = const("cols", [2, N_COLS])
        cv, cs = const("cv", [KT * 2]), const("cs", [KT * 2])
        epsc = const("epsc", [1])
        negmax, sums, sink_e = const("negmax", [4]), const("sums", [4]), const("sink_e", [4])
        rowmax, recip = const("rowmax", [4]), const("recip", [4])
        tot, dec = const("tot", [NB]), const("dec", [NB])
        nsink = const("nsink", [B_HEADS])
        cos_t, sin_t, rot_t = tab[:, 0:SEQ], tab[:, SEQ:2 * SEQ], tab[:, 2 * SEQ:2 * SEQ + P]

        slot = [ctx.enter_context(nc.psum_tensor(f"slot{k}", [P, 1024], f32)) for k in range(4)]
        x_kept = nc.dram_tensor("x_kept", [P, KT, T], f32, kind="Internal").ap()

        def sig(name, **kw):
            return Signal(ctx.enter_context(nc.semaphore(name)), **kw)

        raw_full = [sig(f"raw_full{k}", unit=16, half=True) for k in range(2)]
        ada_full = [sig(f"ada_full{k}", unit=16, half=True) for k in range(2)]
        ada_first_full = [sig(f"ada_first_full{k}", unit=16) for k in range(2)]
        ada_c_full = [sig(f"ada_c_full{k}", unit=16) for k in range(2)]
        ada_read = sig("ada_read")
        high_done, low_done = sig("high_done"), sig("low_done")
        job_done, gate_done = sig("job_done"), sig("gate_done")
        gate_read, z_read = sig("gate_read", credit=2), sig("z_read", credit=2)
        ff_read = sig("ff_read", credit=2)
        act_own, dve_own = sig("act_own"), sig("dve_own")
        consts_in, tab_in, small_in = sig("consts_in", unit=16), sig("tab_in", unit=16), sig("small_in", unit=16)
        x_in, x_saved, out_saved = sig("x_in", unit=16), sig("x_saved", unit=16), sig("out_saved", unit=16)
        init_done, cs_ready, silu_e = sig("init_done"), sig("cs_ready"), sig("silu_e")
        nsink_ready = sig("nsink_ready")
        mod_t_ready, mod_done = sig("mod_t_ready"), sig("mod_done")
        mod_read, gain_ready = sig("mod_read"), sig("gain_ready")
        x_squared, part_summed = sig("x_squared"), sig("part_summed")
        squared, sum_done, ln_read, rstd_ready = sig("squared"), sig("sum_done"), sig("ln_read"), sig("rstd_ready")
        scaled, h_high, h_ready, x_updated = sig("scaled"), sig("h_high"), sig("h_ready"), sig("x_updated")
        copied, r_read, tr_done = sig("copied"), sig("r_read"), sig("tr_done")
        normed, rot_done, rot_read, roped = sig("normed"), sig("rot_done"), sig("rot_read"), sig("roped")
        proj_done = sig("proj_done")
        scores_done, max_ready, exp_ready, prob_ready = sig("scores_done"), sig("max_ready"), sig("exp_ready"), sig("prob_ready")
        prob_t, pt_ready, o_done, y_high, y_low = sig("prob_t"), sig("pt_ready"), sig("o_done"), sig("y_high"), sig("y_low")
        z_done, abs_ready, la_read = sig("z_done"), sig("abs_ready"), sig("la_read")
        diff_ready, e_ready, q_ready, k_ready, zeroed = sig("diff_ready"), sig("e_ready"), sig("q_ready"), sig("k_ready"), sig("zeroed")
        lvl_done, lvl_read, acc_first = sig("lvl_done"), sig("lvl_read"), sig("acc_first")
        inter_e, inter_qk, kt_done, kt_copied, ds_done, state_ready = (sig("inter_e"), sig("inter_qk"), sig("kt_done"),
                                                                      sig("kt_copied"), sig("ds_done"), sig("state_ready"))
        oc_done, oc_read, y_full, sil_ready = sig("oc_done"), sig("oc_read"), sig("y_full"), sig("sil_ready")
        merged, m_high, m_low = sig("merged"), sig("m_high"), sig("m_low")
        relu_ready, u_high, u_low = (sig(n, half=True) for n in ("relu_ready", "u_high", "u_low"))
        out_ready = sig("out_ready")

        block = ctx.enter_context(nc.Block())

        def queries(layer):
            return T if layer < DEPTH - 1 else SEQ

        def chunks(n):
            return ((0, SEQ), (SEQ, T)) if n == T else ((0, SEQ),)

        def sides(n):
            return ((0, SEQ, 0), (SEQ, T, 1)) if n == T else ((0, SEQ, 0),)

        def col(layer, name, k=0):
            return cols[:, layer, COL[name] + k:COL[name] + k + 1]

        COPIES = {b: sum({"r": 0, "v": 2}.get(kind, 1) for kind, _ in PROJ[b]) for b in BRANCHES}
        COPIES["A"] += A_HEADS + A_HEADS // 2 + A_HEADS + NB
        OTHER_COPIES = sum(COPIES[b] for b in BRANCHES[1:])

        def attention_tiles(branch, layer):
            tiles = []
            nq = queries(layer) // P
            if branch == "B":
                for g in range(B_KV):
                    for n in range(nq):
                        keys = [m for m in (n - 1, n, n + 1) if 0 <= m < LB] if n < LB else []
                        for j in range(B_GROUP):
                            tiles.append(dict(last=j == B_GROUP - 1, first=j == 0, g=g, j=j, n=n, keys=keys + list(range(LB, NB)),
                                              lat=len(keys), col=j * P, width=B_GROUP * P))
            else:
                for h in range(4):
                    for blocks, keys in ((range(LB), range(NB)), (range(LB, NB), range(LB, NB))):
                        if blocks[0] >= nq:
                            continue
                        for n in blocks:
                            tiles.append(dict(last=n == blocks[-1], first=n == blocks[0], h=h, n=n, keys=list(keys),
                                              col=(n - blocks[0]) * P, width=len(blocks) * P, q0=blocks[0] * P))
            return tiles

        def outputs(branch, layer):
            return C_HEADS if branch == "C" else sum(t["last"] for t in attention_tiles(branch, layer))

        def score_span(branch, tile):
            if branch == "B":
                return SEQ - tile["lat"] * P, T
            return (0, T) if len(tile["keys"]) == NB else (SEQ, T)

        def key_units(tile):
            n = len(tile["keys"])
            return [(x, min(x + 3, n)) for x in range(0, n, 3)]

        def unit_bank(u):
            return slot[2 + u % 3 // 2][:, 512 * (u % 3 != 0):512 * (1 + (u % 3 != 0))]

        EARLY = next(n for n, (kind, j) in enumerate(PROJ["C"]) if kind == "v")
        EARLY_COPIES = sum(kind != "r" for kind, _ in PROJ["C"][:EARLY])

        def decay_slot(h):
            return slot[0 if h else 1]

        LAG = 3
        EXP_AND_LN = "natural_log_exp_and_others"
        SCALE = {"A": (A_NOPE + A_ROPE) ** -0.5, "B": B_HD ** -0.5, "D": D_HD ** -0.5}
        PB = {"A": [XS[:, k, :] for k in range(3)] + [SS[:, 9, :]], "B": [SS[:, 3 + k, :] for k in range(4)], "D": [SS[:, 3 + k, :] for k in range(4)]}
        PT = {"A": at("PT_A", [NB, SEQ], f32, (R_S + 4) * ROW), "B": at("PT_B", [NB, SEQ], f32, (R_S + 7) * ROW)}
        PT["D"] = PT["B"]
        QB, KB = XS[:, 1:5, :], XS[:, 0, :]
        KD = at("KD", [2, T], f32, (R_X + 4) * ROW)
        VT = {"C": [XS[:, 4, :], XS[:, 5, :]], "B": [XS[:, 6, :], XS[:, 6, :]], "D": [XS[:, 6, :], XS[:, 7, :]]}
        VB = at("VB", [NB, P], f32, (R_X + 5) * ROW)
        la, cumx, cumy = SS[:, 0, :], SS[:, 1, :], SS[:, 2, :]
        diff, ee = [SS[:, 3, :], XS[:, 4, :]], [SS[:, 4, :], XS[:, 5, :]]
        ks, qs = [SS[:, 5, :], XS[:, 6, :]], [SS[:, 6, :], XS[:, 7, :]]
        acc, qi, ki, kit = SS[:, 7, :], SS[:, 8, :], SS[:, 9, :], SS[:, 10, :]
        state = at("state", [NB, P], f32, (R_S + 11) * ROW)

        def level_buffer(n):
            return (n + 1) % 2

        QR, KN = XS[:, 3:5, :], [XS[:, 5, :], XS[:, 6, :], XS[:, 7, :], SS[:, 8, :]]
        KR = SS[:, 11, :]
        SQ = {"A": [SS[:, 9, :], SS[:, 10, :]], "D": [SS[:, 0, :], SS[:, 1, :]]}
        RSTD = {"A": [XS[:, 5, :], XS[:, 6, :]], "D": [SS[:, 2, :], SS[:, 3, :]]}
        ROT = {"A": SS[:, 10, :], "B": SS[:, 11, :], "D": SS[:, 11, :]}

        def rotated(branch, kind, j):
            if branch == "B":
                return QB[:, j, :] if kind == "q" else KB
            return QY[:, j, :] if kind == "q" else KD[:, j, :]

        def flat1(ap):
            return ap.rearrange("p (a t) -> p a t", a=1)

        def output_parts(branch, tile, dst):
            if branch == "B":
                g, n = tile["g"], tile["n"]
                src = slot[3][0:B_HD, 0:tile["width"]].rearrange("p (a o s) -> p o a s", o=2, s=P)
                return [(dst[odd * B_HD:(odd + 1) * B_HD, 2 * g:2 * g + 2, n * P:(n + 1) * P], src[:, odd, :, :]) for odd in range(2)]
            return [(dst[:, tile["h"], tile["q0"]:tile["q0"] + tile["width"]], slot[3][:, 0:tile["width"]])]

        SIZES = []
        for b in BRANCHES:
            SIZES += [KT] * N_PROJ[b] + [WIDE] * KT
        SIZES += [KT] * (KT + 2 * FF_GROUPS * KT)
        N_JOBS = len(SIZES)
        ADA_STEPS = list(range(0, KT, KT // ADA_PER_GROUP))

        @block.sync
        def _(sp):
            def tile(src, dst, full, p, size):
                sp.dma_start(dst[p][:, 0:size, :], src).then_inc(full[p].sem, 16)

            for dst, src in ((cv[:, :], cvec), (cols[:, :, :], cols_d), (ident[:, :], const_d[:, 0:P]),
                             (glamask[:, :, :], glamask_d), (winmask[:, :, :], winmask_d)):
                sp.dma_start(dst, src).then_inc(consts_in.sem, 16)
            for k in range(2):
                sp.dma_start(ada_first[k][:, :, :, :], w_ada[k * (ADA_FIRST // 2):(k + 1) * (ADA_FIRST // 2)].rearrange("t p k n -> p t k n")).then_inc(ada_first_full[k].sem, 16)
            at8 = at12 = jobs = 0
            ada = ADA_FIRST
            first = True
            for layer in range(DEPTH):
                for section in BRANCHES + "M":
                    parts = ([(w8, N_PROJ[section], KT), (w12, KT, WIDE)] if section in BRANCHES
                             else [(w8, KT + 2 * FF_GROUPS * KT, KT)])
                    for src, n, size in parts:
                        start = at8 if src is w8 else at12
                        k = 0
                        while first and k < 2:
                            tile(src[start + k], raw, raw_full, (jobs + k) % 2, size)
                            k += 1
                        first = False
                        if src is w12 and section == BRANCHES[0]:
                            while k < 2:
                                sp.wait_ge(low_done.sem, jobs + k - 1)
                                tile(src[start + k], raw, raw_full, (jobs + k) % 2, size)
                                k += 1
                            sp.wait_ge(job_done.sem, jobs)
                            with sp.Fori(0, C_HEADS * ADA_PER_HEAD // 2) as turn:
                                for x in range(2):
                                    sp.wait_ge(ada_read.sem, turn * 2 + (ada + x - 1))
                                    tile(w_ada[turn * 2 + (ada + x)], ada_c_raw, ada_c_full, x, KT)
                            ada += ADA_TILES
                        turns = (n - k) // 2
                        if turns > 1:
                            with sp.Fori(0, turns) as turn:
                                for x in range(2):
                                    sp.wait_ge(low_done.sem, turn * 2 + (jobs + k + x - 1))
                                    tile(src[turn * 2 + (start + k + x)], raw, raw_full, (jobs + k + x) % 2, size)
                            k += 2 * turns
                        while k < n:
                            sp.wait_ge(low_done.sem, jobs + k - 1)
                            tile(src[start + k], raw, raw_full, (jobs + k) % 2, size)
                            k += 1
                        jobs += n
                        if src is w8:
                            at8 += n
                        else:
                            at12 += n
            for k in range(KT):
                sp.wait_ge(out_ready.sem, k + 1)
                sp.dma_start(out[:, k, :], M[:, k, 0:SEQ]).then_inc(out_saved.sem, 16)
            sp.wait_ge(out_saved.sem, 16 * KT)

        @block.gpsimd
        def _(pool):
            w = Counts(pool)
            def modulation_tiles(first):
                with pool.Fori(0, ADA_FIRST // 2) as turn:
                    for k in range(2):
                        pool.wait_ge(ada_read.sem, turn * 2 + (first + k - 1))
                        pool.dma_start(ada_raw[k][:, :, :], w_ada[turn * 2 + (first + k)]).then_inc(ada_full[k].sem, 16)

            def tables(b, layer):
                if b == "C":
                    pool.dma_start(tab[64:64 + 2 * C_RANK, 0:C_HEADS * P], wdec_d[layer]).then_inc(tab_in.sem, 16)
                else:
                    pool.dma_start(tab[:, :], tabs_d[1 if b == "D" else 0]).then_inc(tab_in.sem, 16)
                if b == "A":
                    pool.dma_start(w_small[:, :], small_d[layer]).then_inc(small_in.sem, 16)

            for layer in range(DEPTH):
                nq = queries(layer)
                if layer == 0:
                    pool.dma_start(X[:, :, :], xT).then_inc(x_in.sem, 16)
                else:
                    pool.wait_ge(ff_read.sem, w.next(ff_read, 2 * FF_GROUPS * KT))
                    pool.dma_start(x_kept, X[:, :, :]).then_inc(x_saved.sem, 16)
                    pool.wait_ge(x_saved.sem, w.next(x_saved))
                tables("C", layer)
                for b, after in zip(BRANCHES, BRANCHES[1:] + "M"):
                    if b == "C":
                        pool.wait_ge(copied.sem, w.next(copied, COPIES["C"] + (OTHER_COPIES if layer else 0)))
                        for h in range(C_HEADS):
                            for n, m in enumerate(LEVELS):
                                if n >= 2:
                                    pool.wait_ge(lvl_done.sem, w.next(lvl_done, 2 if n == 3 else 1))
                                elif h > 0:
                                    if n == 0:
                                        pool.wait_ge(lvl_done.sem, w.next(lvl_done, 2))
                                pool.memset(qs[level_buffer(n)][:, 0:nq], 0.0).then_inc(zeroed.sem, 1)
                                pool.wait_ge(e_ready.sem, w.next(e_ready))
                                pool.tensor_tensor(ks[level_buffer(n)][:, 0:nq], kk[:, h, 0:nq], ee[level_buffer(n)][:, 0:nq], ALU.mult).then_inc(k_ready.sem, 1)
                        pool.wait_ge(lvl_done.sem, w.next(lvl_done, 2))
                    pool.wait_ge(y_low.sem, w.next(y_low, outputs(b, layer)))
                    if after != "M":
                        tables(after, layer)
                    else:
                        pool.dma_start(X[:, :, :], xT if layer == 0 else x_kept).then_inc(x_in.sem, 16)
                if layer < DEPTH - 1:
                    modulation_tiles((layer + 1) * ADA_TILES)

        @block.tensor
        def _(pe):
            w, slots = Counts(pe), Slots(init_done)
            jobs = [0]

            def mm(dst, lhsT, rhs, start=True, stop=True):
                return pe.matmul(dst, lhsT, rhs, start=start, stop=stop)

            def split_product(dst, w_high, w_low, x_high, x_low, n, kts, per_k=None, w_at=0):
                for k in range(kts):
                    if per_k is not None:
                        pe.wait_ge(per_k.sem, w.next(per_k))
                    for a, (wp, xp) in enumerate(((w_high, x_high), (w_high, x_low), (w_low, x_high))):
                        for lo, hi in chunks(n):
                            last = mm(dst[:, lo:hi], wp[:, w_at + k, :], xp[:, k, lo:hi],
                                      start=k == 0 and a == 0, stop=k == kts - 1 and a == 2)
                return last

            def job(x_high, x_low, n, release, per_k=None, x=None, modulate=None):
                p = jobs[0] % 2
                pe.wait_ge(low_done.sem, w.next(low_done))
                if x is None:
                    pe.wait_ge(*slots.next(2 * p, release))
                else:
                    pe.wait_ge(release.sem, slots.job_before_last(w, x, release))
                if modulate is not None:
                    modulation_in(2 * p, ada_full[modulate], ada_raw[modulate])
                split_product(slot[2 * p], wh[p], wl[p], x_high, x_low, n, KT, per_k).then_inc(job_done.sem, 1)
                jobs[0] += 1

            def first_modulation():
                pe.wait_ge(*slots.next(2, mod_t_ready))
                pe.wait_ge(*slots.next(3, mod_t_ready))
                per_bank = SEQ // P
                for n in range(ADA_FIRST // per_bank):
                    half, t = divmod(n * per_bank, ADA_FIRST // 2)
                    if t == 0:
                        pe.wait_ge(ada_first_full[half].sem, w.next(ada_first_full[half]))
                    dst = slot[2 + n // 2][0:2, (n % 2) * SEQ:(n % 2 + 1) * SEQ].rearrange("p (a s) -> p a s", s=P)
                    for k in range(KT):
                        last = mm(dst, cs[:, 2 * k:2 * k + 2], ada_first[half][:, t:t + per_bank, k, :], start=k == 0, stop=k == KT - 1)
                    last.then_inc(ada_read.sem, per_bank)

            def modulation_in(where, full, tile):
                pe.wait_ge(full.sem, w.next(full))
                for k in range(KT):
                    last = mm(slot[where][0:2, T:T + P], cs[:, 2 * k:2 * k + 2], tile[:, k, :], start=k == 0, stop=k == KT - 1)
                last.then_inc(ada_read.sem, 1)

            def modulation_columns(src, n):
                pe.wait_ge(*slots.next(3, mod_read))
                for t in range(n):
                    last = mm(slot[3][:, 2 * t:2 * t + 2], src[0:2, t * P:(t + 1) * P], ident[0:2, 0:2])
                last.then_inc(mod_done.sem, 1)

            def ones_sum(where, src, n, release, first=True, last=True):
                if first:
                    pe.wait_ge(*slots.next(where, release))
                for lo, hi in chunks(n):
                    ins = mm(slot[where][:, lo:hi], ones[:, :], src[:, lo:hi], start=first, stop=last)
                return ins

            def norm_sum(n):
                pe.wait_ge(x_squared.sem, w.next(x_squared, KT))
                pe.wait_ge(part_summed.sem, w.next(part_summed, KT - 2))
                ones_sum(1, tmp[:, 3, :], n, ln_read, True, False)
                ones_sum(1, tmp[:, (KT - 1) % 2, :], n, ln_read, False, True).then_inc(sum_done.sem, 1)

            def transposes(where, src, blocks, release):
                pe.wait_ge(*slots.next(where, release))
                for n in range(blocks):
                    last = pe.transpose(slot[where][:, n * P:(n + 1) * P], src[:, n * P:(n + 1) * P], ident[:, :])
                return last

            def rotate(where, src, parts=P):
                pe.wait_ge(*slots.next(where, rot_read))
                mm(slot[where][0:parts, 0:SEQ], rot_t[0:parts, 0:parts], src[0:parts, 0:SEQ]).then_inc(rot_done.sem, 1)

            def decay_logits(h):
                pe.wait_ge(*slots.next(0 if h else 1, la_read))
                for lo, hi in chunks(T):
                    last = mm(decay_slot(h)[:, lo:hi], tab[64:64 + 2 * C_RANK, h * P:(h + 1) * P], misc[64:64 + 2 * C_RANK, lo:hi])
                last.then_inc(z_done.sem, 1)

            def project(branch, nq):
                plan = PROJ[branch]
                for n in range(len(plan) + 1):
                    if n < len(plan):
                        kind = plan[n][0]
                        narrow = kind in ("r", "q", "cq")
                        job(Hh, Hl, nq if narrow else T, r_read if kind == "r" else copied, per_k=h_ready if branch == "C" and n == 0 else None)
                    if n == 0:
                        continue
                    if branch == "C" and n == EARLY:
                        pe.wait_ge(copied.sem, w.next(copied, EARLY_COPIES))
                        pe.wait_ge(tab_in.sem, w.next(tab_in))
                        decay_logits(0)
                    kind, j = plan[n - 1]
                    beside = 1 + 2 * ((n - 1) % 2)
                    if kind == "v":
                        pe.wait_ge(copied.sem, slots.declared[copied] - (n < len(plan)))
                        transposes(beside, VT[branch][j % 2], NB, copied).then_inc(tr_done.sem, 1)
                    elif branch == "B":
                        pe.wait_ge(copied.sem, slots.declared[copied] - 1)
                        rotate(beside, rotated(branch, kind, j))
                    elif branch == "D":
                        pe.wait_ge(squared.sem, w.next(squared))
                        ones_sum(beside, SQ["D"][(n - 1) % 2], nq if kind == "q" else T, ln_read).then_inc(sum_done.sem, 1)
                    elif branch == "A":
                        pe.wait_ge(squared.sem, w.next(squared))
                        if kind == "cq":
                            ones_sum(1, SQ["A"][j], nq, ln_read, j == 0, j == 1).then_inc(sum_done.sem, 1)
                        else:
                            ones_sum(3, SQ["A"][0], T, ln_read).then_inc(sum_done.sem, 1)
                    if branch == "D" and n >= 2 and plan[n - 2][0] in "qk":
                        pe.wait_ge(normed.sem, w.next(normed))
                        rotate(1 + 2 * (n % 2), rotated(branch, *plan[n - 2]))

            def branch_c(nq):
                nc_q = nq // P
                pe.wait_ge(copied.sem, w.next(copied, COPIES["C"] - EARLY_COPIES))

                def output(h):
                    pe.wait_ge(state_ready.sem, w.next(state_ready))
                    pe.wait_ge(lvl_read.sem, w.next(lvl_read, len(LEVELS)))
                    pe.wait_ge(*slots.next(1, oc_read))
                    for c in range(nc_q):
                        s = slice(c * P, (c + 1) * P)
                        mm(slot[1][:, s], state[:, c, :], qi[:, s], start=True, stop=False)
                        last = mm(slot[1][:, s], V[:, h, s], acc[:, s], start=False, stop=True)
                    last.then_inc(oc_done.sem, 1)
                    modulation_columns(mod_c_t, ADA_PER_HEAD)
                    pe.wait_ge(squared.sem, w.next(squared))
                    ones_sum(0, kit, nq, ln_read).then_inc(sum_done.sem, 1)

                for h in range(C_HEADS):
                    if h > 0:
                        output(h - 1)
                    pe.wait_ge(inter_qk.sem, w.next(inter_qk))
                    transposes(0, ki, NB, kt_copied).then_inc(kt_done.sem, 1)
                    for n in range(len(LEVELS) + 1):
                        if n == len(LEVELS) and h + 1 < C_HEADS:
                            decay_logits(h + 1)
                        where = 2 + n % 2
                        pe.wait_ge(*slots.next(where, acc_first if n == 0 else lvl_read))
                        if n > 0:
                            modulation_in(where, ada_c_full[n % 2], ada_c_raw[n % 2])
                        if n == 1:
                            left, right = kk[:, h, :], qq[:, h, :]
                        else:
                            pe.wait_ge(k_ready.sem, w.next(k_ready))
                            pe.wait_ge(q_ready.sem, w.next(q_ready))
                            buffer = level_buffer(max(n - 1, 0))
                            left, right = ks[buffer], qs[buffer]
                        for c in range(nc_q):
                            s = slice(c * P, (c + 1) * P)
                            last = mm(slot[where][:, s], left[:, s], right[:, s])
                        last.then_inc(lvl_done.sem, 1)
                        if n == 0:
                            pe.wait_ge(*slots.next(1, state_ready))
                            modulation_in(1, ada_c_full[0], ada_c_raw[0])
                            pe.wait_ge(kt_copied.sem, w.next(kt_copied))
                            for c in range(NB):
                                s = slice(c * P, (c + 1) * P)
                                last = mm(slot[1][:, s], kit[:, s], V[:, h, s])
                            last.then_inc(ds_done.sem, 1)
                output(C_HEADS - 1)
                slots.declared[y_low] = slots.declared.get(y_low, 0) + C_HEADS

            def branch_a(nq):
                pe.wait_ge(small_in.sem, w.next(small_in))
                pe.wait_ge(tab_in.sem, w.next(tab_in))
                rotate(1, misc, A_ROPE)
                pe.wait_ge(normed.sem, w.next(normed, 2))
                order = [(None, h) for h in range(A_HEADS)] + [("rope", j) for j in range(2)]
                for n, (kind, h) in enumerate(order):
                    where = 2 * (n % 2)
                    pe.wait_ge(*slots.next(where, copied))
                    block_at = h if kind is None else A_HEADS + h
                    for k in range(2):
                        for lo, hi in chunks(nq):
                            last = mm(slot[where][:, lo:hi], w_uq[:, k, block_at * P:(block_at + 1) * P], XS[:, k, lo:hi],
                                      start=k == 0, stop=k == 1)
                    last.then_inc(proj_done.sem, 1)
                pe.wait_ge(normed.sem, w.next(normed))
                for h in range(A_HEADS):
                    where = 2 * (h % 2)
                    pe.wait_ge(*slots.next(where, copied))
                    for lo, hi in chunks(T):
                        last = mm(slot[where][:, lo:hi], w_ukv[:, h, :], XS[:, 2, lo:hi])
                    last.then_inc(proj_done.sem, 1)
                for n in range(NB):
                    where = 2 * (n % 2)
                    pe.wait_ge(*slots.next(where, copied))
                    mm(slot[where][:, 0:A_HEADS * A_V], XS[:, 2, n * P:(n + 1) * P],
                       w_ukv[:, A_HEADS:2 * A_HEADS, :]).then_inc(proj_done.sem, 1)
                pe.wait_ge(copied.sem, w.next(copied, COPIES["A"]))
                for j in range(2):
                    rotate(1 + 2 * j, QR[:, j, :])
                pe.wait_ge(roped.sem, w.next(roped, 4))

            def attention(branch, layer):
                tiles = attention_tiles(branch, layer)
                values_in = units = 0
                pe.wait_ge(*slots.last(2))
                pe.wait_ge(*slots.last(3))
                for n in range(3):
                    slots.held["unit", n] = slots.last(2)
                for i in range(len(tiles) + LAG + 1):
                    if i < len(tiles):
                        tile = tiles[i]
                        out_s = slot[i % 2]
                        pe.wait_ge(*slots.next(i % 2, exp_ready))
                        a, b = score_span(branch, tile)
                        n = tile["n"]
                        qs_ = slice(n * P, (n + 1) * P)
                        if branch == "B":
                            g, j = tile["g"], tile["j"]
                            part = slice(g * B_HD, (g + 1) * B_HD)
                            q = QB[part, j, qs_]
                            for x, m in enumerate(tile["keys"][:tile["lat"]]):
                                dst = out_s[:, a + x * P:a + (x + 1) * P]
                                edge = m != n
                                mm(dst, q, KB[part, m * P:(m + 1) * P], start=True, stop=not edge)
                                if edge:
                                    mm(dst, ident[:, :], winmask[:, 0 if m < n else 1, :], start=False, stop=True)
                            last = mm(out_s[:, SEQ:T], q, KB[part, SEQ:T])
                        else:
                            h = tile["h"]
                            for lo, hi in ((0, SEQ), (SEQ, T)):
                                if hi <= a:
                                    continue
                                if branch == "A":
                                    part = slice((h % 2) * A_ROPE, (h % 2 + 1) * A_ROPE)
                                    mm(out_s[:, lo:hi], QY[:, h, qs_], KN[h][:, lo:hi], start=True, stop=False)
                                    last = mm(out_s[:, lo:hi], QR[part, h // 2, qs_], KR[part, lo:hi], start=False, stop=True)
                                else:
                                    last = mm(out_s[:, lo:hi], QY[:, h, qs_], KD[:, h // (D_HEADS // D_KV), lo:hi])
                        last.then_inc(scores_done.sem, 1)
                    if i > LAG and tiles[i - LAG - 1]["last"]:
                        tile = tiles[i - LAG - 1]
                        pe.wait_ge(pt_ready.sem, w.next(pt_ready, values_in))
                        values_in = 0
                        pe.wait_ge(*slots.next(3, y_low))
                        for x, m in enumerate(tile["keys"]):
                            pt = PT[branch][:, x, 0:tile["width"]]
                            flags = dict(start=x == 0, stop=x == len(tile["keys"]) - 1)
                            if branch == "B":
                                g = tile["g"]
                                last = mm(slot[3][0:B_HD, 0:tile["width"]], VB[:, m, g * B_HD:(g + 1) * B_HD], pt, **flags)
                            elif branch == "A":
                                values = VA[:, :, :].rearrange("p a t -> p (a t)")[:, m * SEQ + tile["h"] * P:m * SEQ + (tile["h"] + 1) * P]
                                last = mm(slot[3][:, 0:tile["width"]], values, pt, **flags)
                            else:
                                last = mm(slot[3][:, 0:tile["width"]], V[:, tile["h"] // 2, m * P:(m + 1) * P], pt, **flags)
                        last.then_inc(o_done.sem, 1)
                    if LAG <= i < len(tiles) + LAG:
                        tile = tiles[i - LAG]
                        pe.wait_ge(prob_ready.sem, w.next(prob_ready))
                        probs = PB[branch][(i - LAG) % (LAG + 1)]
                        for lo, hi in key_units(tile):
                            pe.wait_ge(*slots.next(("unit", units % 3), pt_ready))
                            for x in range(lo, hi):
                                last = pe.transpose(unit_bank(units)[:, (x - lo) * P:(x - lo + 1) * P], probs[:, x * P:(x + 1) * P], ident[:, :])
                            last.then_inc(prob_t.sem, 1)
                            units += 1
                            values_in += 1
                slots.held[2] = slots.last(("unit", (units - 1) % 3))

            def gates(nq, groups):
                pe.wait_ge(y_low.sem, w.next(y_low, groups))
                pe.wait_ge(*slots.last(0))
                pe.wait_ge(*slots.last(1))
                pe.wait_ge(*slots.last(2))
                pe.wait_ge(*slots.last(3))

                def gate_job(x):
                    p = jobs[0] % 2
                    pe.wait_ge(low_done.sem, w.next(low_done))
                    if x is not None:
                        pe.wait_ge(gate_read.sem, slots.job_before_last(w, x, gate_read))
                    else:
                        pe.wait_ge(*slots.next(2 * p, gate_read))
                    split_product(slot[2 * p], wh[p], wl[p], Hh, Hl, nq, KT).then_inc(gate_done.sem, 1)
                    if x is not None:
                        pe.wait_ge(z_read.sem, slots.job_before_last(w, x, z_read))
                    else:
                        pe.wait_ge(*slots.next(2 * p + 1, z_read))
                    split_product(slot[2 * p + 1], wh[p], wl[p], Yh, Yl, nq, BK, w_at=KT).then_inc(job_done.sem, 1)
                    jobs[0] += 1

                turns = KT // 2 - 1
                p = jobs[0] % 2
                with w.loop(turns, 2):
                    for x in range(2):
                        gate_job(x)
                slots.after_loop(gate_read, 2 * turns, (2 * p, 2 * (1 - p)))
                slots.after_loop(z_read, 2 * turns, (2 * p + 1, 2 * (1 - p) + 1))
                for x in range(2):
                    gate_job(None)

            def mlp(nq, ada):

                def hidden(x, loop):
                    n = ADA_STEPS.index(x) % 2 if ada and x in ADA_STEPS else None
                    job(Hh, Hl, nq, ff_read, per_k=h_ready if loop == "first" and x == 0 else None, x=x if loop == "loop" else None, modulate=n)

                def back(x, loop):
                    job(Uh, Ul, nq, ff_read, per_k=u_low if x == 0 else None, x=KT + x if loop == "loop" else None)

                def group(loop):
                    for x in range(KT):
                        hidden(x, loop)
                    for x in range(KT):
                        back(x, loop)

                group("first")
                p = jobs[0] % 2
                with w.loop(FF_GROUPS - 2, 2 * KT, {s: ADA_PER_GROUP // 2 for s in ada_full}):
                    group("loop")
                slots.after_loop(ff_read, (FF_GROUPS - 2) * 2 * KT, (2 * p, 2 * (1 - p)))
                group("last")
                norm_sum(nq)
                if ada:
                    pe.wait_ge(*slots.last(0))
                    pe.wait_ge(*slots.last(2))
                    modulation_columns(mod_first_t, ADA_FIRST)

            pe.wait_ge(consts_in.sem, w.next(consts_in, 5))
            pe.wait_ge(init_done.sem, w.next(init_done))
            pe.wait_ge(cs_ready.sem, w.next(cs_ready))
            for layer in range(DEPTH):
                nq = queries(layer)
                if layer == 0:
                    first_modulation()
                    pe.wait_ge(mod_t_ready.sem, w.next(mod_t_ready, 2))
                    modulation_columns(mod_first_t, ADA_FIRST)
                    norm_sum(T)
                for b in BRANCHES:
                    if b in "BD":
                        pe.wait_ge(tab_in.sem, w.next(tab_in))
                    project(b, nq)
                    if b == "C":
                        branch_c(nq)
                    if b == "A":
                        branch_a(nq)
                    if b in "BD":
                        pe.wait_ge(copied.sem, w.next(copied, COPIES[b]))
                        pe.wait_ge(roped.sem, w.next(roped, sum(kind != "v" for kind, _ in PROJ[b])))
                    if b != "C":
                        attention(b, layer)
                    gates(nq, outputs(b, layer))
                for k in range(KT):
                    job(Mh, Ml, nq, x_updated, per_k=m_low if k == 0 else None)
                norm_sum(nq)
                mlp(nq, layer < DEPTH - 1)

        @block.scalar
        def _(act):
            w = Counts(act)
            jobs = [0]

            def done(ins):
                ins.then_inc(act_own.sem, 1)
                act.wait_ge(act_own.sem, w.next(act_own))

            def high(n, p):
                act.wait_ge(raw_full[p].sem, w.next(raw_full[p]))
                act.activation(wh[p][:, 0:SIZES[n], :], raw[p][:, 0:SIZES[n], :], ACT.Copy).then_inc(high_done.sem, 1)

            def square(k, n):
                if k == 2 or k >= 4:
                    act.wait_ge(part_summed.sem, w.next(part_summed))
                act.activation(tmp[:, k % 2, 0:n], X[:, k, 0:n], ACT.Square).then_inc(x_squared.sem, 1)

            def begin_job(square_before=None):
                n = jobs[0] % N_JOBS
                if n + 1 < N_JOBS:
                    high(n + 1, (n + 1) % 2)
                if square_before is not None:
                    act.wait_ge(x_updated.sem, w.next(x_updated))
                    square(*square_before)
                act.wait_ge(job_done.sem, w.next(job_done))
                jobs[0] += 1
                return n % 2

            def rsqrt(where, n, dim, rstd, sums_to_take=1):
                act.wait_ge(sum_done.sem, w.next(sum_done, sums_to_take))
                act.activation(rstd[:, 0:n], slot[where][:, 0:n], ACT.Ln, scale=1.0 / dim, bias=epsc[:, 0:1]).then_inc(ln_read.sem, 1)
                act.wait_ge(ln_read.sem, w.next(ln_read))
                act.activation(rstd[:, 0:n], rstd[:, 0:n], ACT.Exp, scale=-0.5).then_inc(rstd_ready.sem, 1)

            def norm(n, gain, shift_at):
                act.wait_ge(part_summed.sem, w.next(part_summed))
                rsqrt(1, n, D_MODEL, tmp[:, 2, :])
                if gain is None:
                    return
                act.wait_ge(gain_ready.sem, w.next(gain_ready))
                for k in range(KT):
                    act.wait_ge(scaled.sem, w.next(scaled))
                    for lo, hi, side in sides(n):
                        done(act.activation(tmp[:, k % 2, lo:hi], tmp[:, k % 2, lo:hi], ACT.Identity,
                                            scale=gain[:, k, side:side + 1], bias=mod[:, shift_at + k, side:side + 1]))
                    act.activation(Hh[:, k, 0:n], tmp[:, k % 2, 0:n], ACT.Copy).then_inc(h_high.sem, 1)

            def decays(layer, h):
                act.wait_ge(z_done.sem, w.next(z_done))
                done(act.activation(diff[0][:, 0:T], decay_slot(h)[:, 0:T], ACT.Abs, bias=col(layer, "c_bias", h)))
                done(act.activation(diff[0][:, 0:T], diff[0][:, 0:T], ACT.Exp, scale=-1.0))
                act.activation(diff[0][:, 0:T], diff[0][:, 0:T], ACT.Ln, bias=1.0).then_inc(abs_ready.sem, 1)

            def project(branch, layer, nq):
                plan = PROJ[branch]

                def copy_out(n, kind, j, s):
                    nn = nq if kind in ("r", "q", "cq") else T
                    if kind == "r":
                        act.activation(QY[:, j, 0:nn], s[:, 0:nn], ACT.Sigmoid).then_inc(sil_ready.sem, 1)
                    elif kind == "misc":
                        act.activation(misc, s[:, 0:T], ACT.Copy).then_inc(copied.sem, 1)
                    elif branch == "C" and kind in "qk":
                        dst, scale = (qq, C_DK ** -0.5) if kind == "q" else (kk, 1.0)
                        for half in range(2):
                            for copy in range(2):
                                ins = act.activation(dst[copy * C_DK:(copy + 1) * C_DK, 2 * j + half, 0:nn],
                                                     s[half * C_DK:(half + 1) * C_DK, 0:nn], ACT.Copy, scale=scale)
                        ins.then_inc(copied.sem, 1)
                    elif kind == "v":
                        act.activation(VT[branch][j % 2], s[:, 0:T], ACT.Copy).then_inc(copied.sem, 1)
                    elif branch == "A":
                        if n == 2:
                            act.wait_ge(sum_done.sem, w.next(sum_done))
                        act.activation(SQ["A"][n % 2][:, 0:nn], s[:, 0:nn], ACT.Square).then_inc(squared.sem, 1)
                        act.activation(XS[:, n, 0:nn], s[:, 0:nn], ACT.Copy).then_inc(copied.sem, 1)
                    elif branch == "B":
                        act.activation(QB[:, j, 0:nn] if kind == "q" else KB[:, 0:nn], s[:, 0:nn], ACT.Copy).then_inc(copied.sem, 1)
                    else:
                        act.activation(SQ["D"][n % 2][:, 0:nn], s[:, 0:nn], ACT.Square).then_inc(squared.sem, 1)
                        act.activation(QY[:, j, 0:nn] if kind == "q" else KD[:, j, 0:nn], s[:, 0:nn], ACT.Copy).then_inc(copied.sem, 1)

                if branch == "C":
                    act.preload_act_table(ACT.Sigmoid)
                for n in range(len(plan) + 1):
                    if n < len(plan):
                        if plan[n][0] == "misc":
                            act.preload_act_table_set(EXP_AND_LN)
                        p = begin_job()
                        copy_out(n, plan[n][0], plan[n][1], slot[2 * p])
                    if branch == "C" and n == EARLY:
                        decays(layer, 0)
                    if n == 0:
                        continue
                    kind, j = plan[n - 1]
                    beside = 1 + 2 * ((n - 1) % 2)
                    if kind == "v":
                        act.wait_ge(tr_done.sem, w.next(tr_done))
                        dst = VB[:, :, :].rearrange("p a t -> p (a t)") if branch == "B" else V[:, j, :]
                        act.activation(dst, slot[beside][:, 0:T], ACT.Copy).then_inc(copied.sem, 1)
                    elif branch == "D":
                        if n > 2:
                            act.wait_ge(normed.sem, w.next(normed))
                        rsqrt(beside, nq if kind == "q" else T, D_HD, RSTD["D"][(n - 1) % 2])
                if branch == "A":
                    rsqrt(1, nq, A_Q_RANK, RSTD["A"][0], 1)
                    rsqrt(3, T, A_KV_RANK, RSTD["A"][1], 1)
                if branch == "D":
                    act.wait_ge(normed.sem, w.next(normed, 2))

            def branch_c(layer, nq):
                f, b = slice(0, C_DK), slice(C_DK, P)

                def norm_factors():
                    act.wait_ge(oc_done.sem, w.next(oc_done))
                    act.activation(kit[:, 0:nq], slot[1][:, 0:nq], ACT.Square).then_inc(squared.sem, 1)
                    rsqrt(0, nq, C_DV, kit)

                def output_high(h):
                    act.wait_ge(y_full.sem, w.next(y_full))
                    act.activation(Yh[:, h, 0:nq], QY[:, h, 0:nq], ACT.Copy).then_inc(y_high.sem, 1)

                def levels_over():
                    act.wait_ge(lvl_done.sem, w.next(lvl_done, len(LEVELS)))
                    act.wait_ge(q_ready.sem, w.next(q_ready, 2))
                    act.wait_ge(k_ready.sem, w.next(k_ready, 2))

                for h in range(C_HEADS):
                    if h > 0:
                        norm_factors()
                        levels_over()
                    act.wait_ge(diff_ready.sem, w.next(diff_ready))
                    act.activation(ee[0][f, 0:T], cumy[f, 0:T], ACT.Exp, scale=1.0 / C_TEMP)
                    act.activation(ee[0][b, 0:T], diff[0][b, 0:T], ACT.Exp, scale=1.0 / C_TEMP)
                    act.activation(ee[1][f, 0:T], diff[0][f, 0:T], ACT.Exp, scale=1.0 / C_TEMP)
                    act.activation(ee[1][b, 0:T], cumy[b, 0:T], ACT.Exp, scale=1.0 / C_TEMP)
                    act.activation(dec[:, :], tot[:, :], ACT.Exp, scale=1.0 / C_TEMP).then_inc(inter_e.sem, 1)
                    if h > 0:
                        output_high(h - 1)
                    for n, m in enumerate(LEVELS):
                        if n == 0:
                            act.wait_ge(inter_qk.sem, w.next(inter_qk))
                        if n >= 2:
                            act.wait_ge(q_ready.sem, w.next(q_ready))
                            act.wait_ge(k_ready.sem, w.next(k_ready))
                        act.wait_ge(diff_ready.sem, w.next(diff_ready))
                        d = diff[level_buffer(n)][:, 0:nq].rearrange("p (b s) -> p b s", s=2 * m)
                        e = ee[level_buffer(n)][:, 0:nq].rearrange("p (b s) -> p b s", s=2 * m)
                        act.activation(e[:, :, 0:m], d[:, :, 0:m], ACT.Exp, scale=-1.0 / C_TEMP)
                        act.activation(e[:, :, m:2 * m], d[:, :, m:2 * m], ACT.Exp, scale=1.0 / C_TEMP).then_inc(e_ready.sem, 1)
                        if n == 0:
                            act.wait_ge(kt_done.sem, w.next(kt_done))
                            act.activation(kit, slot[0][:, 0:T], ACT.Copy).then_inc(kt_copied.sem, 1)
                        if n == 1:
                            act.wait_ge(lvl_done.sem, w.next(lvl_done))
                            act.activation(acc[:, 0:nq], slot[2][:, 0:nq], ACT.Copy).then_inc(acc_first.sem, 1)
                    if h + 1 < C_HEADS:
                        decays(layer, h + 1)
                norm_factors()
                levels_over()
                output_high(C_HEADS - 1)

            def branch_a(nq):
                order = [("n", h) for h in range(A_HEADS)] + [("rope", j) for j in range(2)]
                for n, (kind, h) in enumerate(order):
                    act.wait_ge(proj_done.sem, w.next(proj_done))
                    act.activation(QY[:, h, 0:nq] if kind == "n" else QR[:, h, 0:nq], slot[2 * (n % 2)][:, 0:nq], ACT.Copy).then_inc(copied.sem, 1)
                act.wait_ge(normed.sem, w.next(normed, 3))
                for h in range(A_HEADS):
                    act.wait_ge(proj_done.sem, w.next(proj_done))
                    act.activation(KN[h], slot[2 * (h % 2)][:, 0:T], ACT.Copy).then_inc(copied.sem, 1)
                va = VA[:, :, :].rearrange("p a t -> p (a t)")
                for n in range(NB):
                    act.wait_ge(proj_done.sem, w.next(proj_done))
                    act.activation(va[:, n * SEQ:(n + 1) * SEQ], slot[2 * (n % 2)][:, 0:SEQ], ACT.Copy).then_inc(copied.sem, 1)

            def attention(branch, layer):
                tiles = attention_tiles(branch, layer)
                units = 0
                for i in range(len(tiles) + LAG + 2):
                    if i - 1 > LAG and tiles[i - LAG - 2]["last"]:
                        act.wait_ge(o_done.sem, w.next(o_done))
                        for hi_, ps in output_parts(branch, tiles[i - LAG - 2], Yh):
                            ins = act.activation(hi_, ps, ACT.Copy)
                        ins.then_inc(y_high.sem, 1)
                    if LAG < i <= len(tiles) + LAG:
                        tile = tiles[i - LAG - 1]
                        for lo, hi in key_units(tile):
                            act.wait_ge(prob_t.sem, w.next(prob_t))
                            act.activation(PT[branch][:, lo:hi, tile["col"]:tile["col"] + P],
                                           unit_bank(units)[:, 0:(hi - lo) * P].rearrange("p (b s) -> p b s", s=P), ACT.Copy).then_inc(pt_ready.sem, 1)
                            units += 1
                    if i < len(tiles):
                        tile = tiles[i]
                        a, b = score_span(branch, tile)
                        s = i % 4
                        act.wait_ge(max_ready.sem, w.next(max_ready))
                        if branch == "B":
                            head = tile["g"] * B_GROUP + tile["j"]
                            act.activation(sink_e[:, s:s + 1], col(layer, "sink", head), ACT.Exp, bias=negmax[:, s:s + 1])
                        act.activation(PB[branch][i % (LAG + 1)][:, 0:b - a], slot[i % 2][:, a:b], ACT.Exp, bias=negmax[:, s:s + 1],
                                       scale=SCALE[branch], accum_out=sums[:, s:s + 1]).then_inc(exp_ready.sem, 1)

            def gates(branch, nq):
                def gate_job(n, x):
                    p = (n + x) % 2
                    high_next(n, x)
                    act.wait_ge(gate_done.sem, w.next(gate_done))
                    act.wait_ge(z_read.sem, w.job_before_last(z_read))
                    act.activation(tmp[:, p, 0:nq], slot[2 * p][:, 0:nq], ACT.Sigmoid).then_inc(gate_read.sem, 1)
                    act.wait_ge(job_done.sem, w.next(job_done))

                def high_next(n, x):
                    if n + x + 1 < N_JOBS:
                        high(n + x + 1, (n + x + 1) % 2)

                n = jobs[0] % N_JOBS
                act.preload_act_table(ACT.Sigmoid)
                with w.loop(KT // 2 - 1, 2):
                    for x in range(2):
                        gate_job(n, x)
                for x in range(KT - 2, KT):
                    gate_job(n, x)
                act.preload_act_table_set(EXP_AND_LN)
                jobs[0] += KT
                if branch == "C":
                    act.wait_ge(z_read.sem, w.taken[z_read, "free"] + z_read.credit)
                else:
                    act.wait_ge(merged.sem, w.next(merged, KT))

            def mlp(nq):
                def group(n, final):
                    def hidden_high(p, j):
                        act.wait_ge(ff_read.sem, w.next(ff_read))
                        act.activation(Uh[:, j, 0:nq], tmp[:, 2 + p, 0:nq], ACT.Copy).then_inc(u_high.sem, 1)

                    for x in range(2 * KT):
                        p = (n + x) % 2
                        if not (final and x == 2 * KT - 1):
                            high_at(n + x + 1)
                        if 0 < x <= KT:
                            hidden_high(1 - p, x - 1)
                        if final and x > KT:
                            act.wait_ge(ff_read.sem, w.next(ff_read))
                            square(x - KT - 1, nq)
                        act.wait_ge(job_done.sem, w.next(job_done))
                        if x < KT:
                            act.activation(tmp[:, p, 0:nq], slot[2 * p][:, 0:nq], ACT.Relu).then_inc(relu_ready.sem, 1)
                    if final:
                        act.wait_ge(ff_read.sem, w.next(ff_read))
                        square(KT - 1, nq)
                    else:
                        act.wait_ge(ff_read.sem, w.next(ff_read, KT))

                def high_at(m):
                    act.wait_ge(raw_full[m % 2].sem, w.next(raw_full[m % 2]))
                    act.activation(wh[m % 2][:, 0:KT, :], raw[m % 2][:, 0:KT, :], ACT.Copy).then_inc(high_done.sem, 1)

                n = jobs[0] % N_JOBS
                with w.loop(FF_GROUPS - 1, 2 * KT):
                    group(n, False)
                group(n, True)
                jobs[0] += 2 * KT * FF_GROUPS

            act.preload_act_table_set(EXP_AND_LN)
            act.wait_ge(consts_in.sem, w.next(consts_in, 5))
            act.wait_ge(init_done.sem, w.next(init_done))
            act.activation(cs[:, :], cv[:, :], ACT.Exp, scale=-1.0).then_inc(silu_e.sem, 1)
            for layer in range(DEPTH):
                nq = queries(layer)
                if layer == 0:
                    act.wait_ge(x_in.sem, w.next(x_in))
                    for k in range(KT):
                        square(k, T)
                high(0, 0)
                norm(T, gain1, MOD_SHIFT1)
                if layer:
                    act.wait_ge(x_saved.sem, w.next(x_saved))
                for b in BRANCHES:
                    project(b, layer, nq)
                    if b == "C":
                        branch_c(layer, nq)
                    if b == "A":
                        branch_a(nq)
                    if b != "C":
                        attention(b, layer)
                    gates(b, nq)
                for k in range(KT):
                    act.activation(Mh[:, k, 0:nq], M[:, k, 0:nq], ACT.Copy).then_inc(m_high.sem, 1)
                for k in range(KT):
                    begin_job((k - 1, nq) if k else None)
                act.wait_ge(x_updated.sem, w.next(x_updated))
                square(KT - 1, nq)
                norm(nq, gain2, MOD_SHIFT2)
                mlp(nq)
            norm(SEQ, None, 0)

        @block.vector
        def _(dve):
            w = Counts(dve)
            jobs = [0]

            def done(ins):
                ins.then_inc(dve_own.sem, 1)
                dve.wait_ge(dve_own.sem, w.next(dve_own))

            def low(n, p=None):
                p = n % 2
                dve.wait_ge(high_done.sem, w.next(high_done))
                dve.tensor_tensor(wl[p][:, 0:SIZES[n], :], raw[p][:, 0:SIZES[n], :], wh[p][:, 0:SIZES[n], :].bitcast(f32),
                                  ALU.subtract).then_inc(low_done.sem, 1)

            def add_squares(k, n):
                dve.wait_ge(x_squared.sem, w.next(x_squared))
                if 0 < k < KT - 1:
                    before = tmp[:, 0, 0:n] if k == 1 else tmp[:, 3, 0:n]
                    dve.tensor_tensor(tmp[:, 3, 0:n], before, tmp[:, k % 2, 0:n], ALU.add).then_inc(part_summed.sem, 1)
                    dve.wait_ge(part_summed.sem, w.next(part_summed))

            def begin_job(squares_before=None):
                n = jobs[0] % N_JOBS
                if n + 1 < N_JOBS:
                    low(n + 1)
                if squares_before is not None:
                    add_squares(*squares_before)
                dve.wait_ge(job_done.sem, w.next(job_done))
                jobs[0] += 1
                return n % 2

            def norm(n, gain, layer):
                dve.wait_ge(rstd_ready.sem, w.next(rstd_ready))
                rstd = tmp[:, 2, 0:n]
                if gain is None:
                    for k in range(KT):
                        dve.scalar_tensor_tensor(out=M[:, k, 0:n], in0=X[:, k, 0:n], scalar=col(layer, "final", k), in1=rstd,
                                                 op0=ALU.mult, op1=ALU.mult).then_inc(out_ready.sem, 1)
                    return

                def low_part(k):
                    dve.wait_ge(h_high.sem, w.next(h_high))
                    dve.tensor_tensor(Hl[:, k, 0:n], tmp[:, k % 2, 0:n], Hh[:, k, 0:n].bitcast(f32), ALU.subtract).then_inc(h_ready.sem, 1)
                    dve.wait_ge(h_ready.sem, w.next(h_ready))

                for k in range(KT):
                    if k >= 2:
                        low_part(k - 2)
                    dve.tensor_tensor(tmp[:, k % 2, 0:n], X[:, k, 0:n], rstd, ALU.mult).then_inc(scaled.sem, 1)
                low_part(KT - 2)
                low_part(KT - 1)

            def rope(row, where, t, parts=P, src=None):
                src = row if src is None else src
                dve.wait_ge(rot_done.sem, w.next(rot_done))
                r = slice(0, parts)
                dve.tensor_tensor(t[r, 0:SEQ], slot[where][r, 0:SEQ], sin_t[r, :], ALU.mult).then_inc(rot_read.sem, 1)
                done(dve.tensor_tensor(row[r, 0:SEQ], src[r, 0:SEQ], cos_t[r, :], ALU.mult))
                dve.wait_ge(rot_read.sem, w.next(rot_read))
                dve.tensor_tensor(row[r, 0:SEQ], row[r, 0:SEQ], t[r, 0:SEQ], ALU.add).then_inc(roped.sem, 1)

            def decay_sums(layer, h):
                f, b = slice(0, C_DK), slice(C_DK, P)
                dve.wait_ge(abs_ready.sem, w.next(abs_ready))
                dve.tensor_scalar(la, decay_slot(h)[:, 0:T], col(layer, "c_bias", h), 0.0, ALU.add, ALU.min).then_inc(la_read.sem, 1)
                dve.wait_ge(la_read.sem, w.next(la_read))
                done(dve.tensor_tensor(la, la, diff[0], ALU.subtract))
                cx = cumx.rearrange("p (b s) -> p b s", s=P)
                lc = la.rearrange("p (b s) -> p b s", s=P)
                dve.memset(cx[:, :, 0:1], 0.0)
                for c in range(NB):
                    ins = dve.tensor_tensor_scan(cx[:, c, 1:P], ones[:, 0:P - 1], lc[:, c, 0:P - 1], 0.0, ALU.mult, ALU.add)
                done(ins)
                dve.tensor_tensor(cumy[f, :], cumx[f, :], la[f, :], ALU.add)
                dve.tensor_copy(cumy[b, :], cumx[b, :])
                done(dve.tensor_tensor(tot[:, :].unsqueeze(2), cx[:, :, P - 1:P], lc[:, :, P - 1:P], ALU.add))
                totb = tot[:, :].unsqueeze(2).to_broadcast([P, NB, P])
                dve.tensor_tensor(diff[0].rearrange("p (b s) -> p b s", s=P), totb, cumy.rearrange("p (b s) -> p b s", s=P),
                                  ALU.subtract).then_inc(diff_ready.sem, 1)

            def project(branch, layer, nq):
                plan = PROJ[branch]
                for n in range(len(plan) + 1):
                    if n < len(plan):
                        p = begin_job()
                        kind, j = plan[n]
                        if kind == "r":
                            dve.wait_ge(sil_ready.sem, w.next(sil_ready))
                            dve.tensor_tensor(QY[:, j, 0:nq], slot[2 * p][:, 0:nq], QY[:, j, 0:nq], ALU.mult).then_inc(r_read.sem, 1)
                    if branch == "C" and n == EARLY:
                        decay_sums(layer, 0)
                    if n > 0 and branch == "D" and plan[n - 1][0] in "qk":
                        kind, j = plan[n - 1]
                        nn = nq if kind == "q" else T
                        row = QY[:, j, 0:nn] if kind == "q" else KD[:, j, 0:nn]
                        dve.wait_ge(rstd_ready.sem, w.next(rstd_ready))
                        dve.scalar_tensor_tensor(out=row, in0=row, scalar=col(layer, "d_" + kind), in1=RSTD["D"][(n - 1) % 2][:, 0:nn],
                                                 op0=ALU.mult, op1=ALU.mult).then_inc(normed.sem, 1)
                    back = 2 if branch == "D" else 1
                    if branch in "BD" and n >= back and plan[n - back][0] in "qk":
                        rope(rotated(branch, *plan[n - back]), 1 + 2 * ((n - back) % 2), ROT[branch])
                        dve.wait_ge(roped.sem, w.next(roped))

            def branch_c(layer, nq):
                f, b = slice(0, C_DK), slice(C_DK, P)
                dve.wait_ge(copied.sem, w.next(copied, COPIES["C"] + (OTHER_COPIES if layer else 0)))
                dve.wait_ge(r_read.sem, w.next(r_read, 4))

                def readout(h):
                    dve.wait_ge(oc_done.sem, w.next(oc_done))
                    dve.wait_ge(rstd_ready.sem, w.next(rstd_ready))
                    dve.tensor_tensor(kit[:, 0:nq], slot[1][:, 0:nq], kit[:, 0:nq], ALU.mult).then_inc(oc_read.sem, 1)
                    dve.wait_ge(oc_read.sem, w.next(oc_read))
                    dve.scalar_tensor_tensor(out=QY[:, h, 0:nq], in0=kit[:, 0:nq], scalar=col(layer, "c_norm"), in1=QY[:, h, 0:nq],
                                             op0=ALU.mult, op1=ALU.mult).then_inc(y_full.sem, 1)
                    modulation_columns(ADA_FIRST + h * ADA_PER_HEAD, ADA_PER_HEAD)

                def output_low(h):
                    dve.wait_ge(y_full.sem, w.next(y_full))
                    dve.wait_ge(y_high.sem, w.next(y_high))
                    dve.tensor_tensor(Yl[:, h, 0:nq], QY[:, h, 0:nq], Yh[:, h, 0:nq].bitcast(f32), ALU.subtract).then_inc(y_low.sem, 1)

                for h in range(C_HEADS):
                    if h > 0:
                        decay_sums(layer, h)

                    def difference(n):
                        m = LEVELS[n]
                        blocks = nq // (2 * m)
                        mid = cumx[:, 0:nq].rearrange("p (b s) -> p b s", s=2 * m)[:, :, m:m + 1].to_broadcast([P, blocks, 2 * m])
                        dve.tensor_tensor(diff[level_buffer(n)][:, 0:nq].rearrange("p (b s) -> p b s", s=2 * m),
                                          cumy[:, 0:nq].rearrange("p (b s) -> p b s", s=2 * m), mid, ALU.subtract).then_inc(diff_ready.sem, 1)

                    def modulation_out(t, src):
                        dve.tensor_copy(mod_c_t[0:2, t * P:(t + 1) * P], src[0:2, T:T + P])

                    def overlay(n):
                        dve.wait_ge(lvl_done.sem, w.next(lvl_done))
                        if n == 1:
                            dve.wait_ge(acc_first.sem, w.next(acc_first))
                        else:
                            dve.wait_ge(lvl_read.sem, w.next(lvl_read))
                        modulation_out(n, slot[2 + n % 2])
                        row = len(LEVELS) - 1 if n == 1 else n - 2
                        mask = glamask[:, row:row + 1, :].bitcast(i32).to_broadcast([P, nq // P, P])
                        dve.copy_predicated(acc[:, 0:nq].rearrange("p (b s) -> p b s", s=P), mask,
                                            slot[2 + n % 2][:, 0:nq].rearrange("p (b s) -> p b s", s=P)).then_inc(lvl_read.sem, 1)

                    difference(0)
                    if h > 0:
                        readout(h - 1)
                    dve.wait_ge(inter_e.sem, w.next(inter_e))
                    dve.tensor_tensor(qi[:, 0:nq], qq[:, h, 0:nq], ee[0][:, 0:nq], ALU.mult)
                    dve.tensor_tensor(ki, kk[:, h, :], ee[1], ALU.mult).then_inc(inter_qk.sem, 1)
                    if h > 0:
                        output_low(h - 1)
                    ds = slot[1][:, 0:T].rearrange("p (b s) -> p b s", s=P)
                    orders = ((f, [LB + c for c in range(NB - LB)] + list(range(LB))),
                              (b, [NB - 1 - c for c in range(NB)]))

                    def state_step(step):
                        for part, order in orders:
                            src, dst = order[step], order[step + 1]
                            if step == 0:
                                ins = dve.tensor_copy(state[part, dst, :], ds[part, src, :])
                            else:
                                ins = dve.scalar_tensor_tensor(out=state[part, dst, :], in0=state[part, src, :], scalar=dec[part, src:src + 1],
                                                               in1=ds[part, src, :], op0=ALU.mult, op1=ALU.add)
                        return ins

                    for n, m in enumerate(LEVELS):
                        if n >= 2:
                            overlay(n - 1)
                        if n + 1 < len(LEVELS):
                            difference(n + 1)
                        dve.wait_ge(e_ready.sem, w.next(e_ready))
                        dve.wait_ge(zeroed.sem, w.next(zeroed))
                        q3 = qs[level_buffer(n)][:, 0:nq].rearrange("p (b s) -> p b s", s=2 * m)
                        e3 = ee[level_buffer(n)][:, 0:nq].rearrange("p (b s) -> p b s", s=2 * m)
                        s3 = qq[:, h, 0:nq].rearrange("p (b s) -> p b s", s=2 * m)
                        dve.tensor_tensor(q3[f, :, m:2 * m], s3[f, :, m:2 * m], e3[f, :, m:2 * m], ALU.mult)
                        dve.tensor_tensor(q3[b, :, 0:m], s3[b, :, 0:m], e3[b, :, 0:m], ALU.mult).then_inc(q_ready.sem, 1)
                        if n == 1:
                            dve.wait_ge(lvl_done.sem, w.next(lvl_done))
                        if n == 2:
                            dve.wait_ge(ds_done.sem, w.next(ds_done))
                            modulation_out(0, slot[1])
                            for part, order in orders:
                                dve.memset(state[part, order[0], :], 0.0)
                        if 2 <= n < NB:
                            done(state_step(n - 2))
                        elif n == NB:
                            state_step(n - 2).then_inc(state_ready.sem, 1)
                    overlay(len(LEVELS) - 1)
                    overlay(len(LEVELS))
                    dve.wait_ge(lvl_read.sem, w.next(lvl_read))
                readout(C_HEADS - 1)
                output_low(C_HEADS - 1)

            def branch_a(layer, nq):
                dve.wait_ge(rstd_ready.sem, w.next(rstd_ready))
                for k in range(2):
                    dve.scalar_tensor_tensor(out=XS[:, k, 0:nq], in0=XS[:, k, 0:nq], scalar=col(layer, "a_q", k), in1=RSTD["A"][0][:, 0:nq],
                                             op0=ALU.mult, op1=ALU.mult).then_inc(normed.sem, 1)
                dve.wait_ge(rstd_ready.sem, w.next(rstd_ready))
                dve.scalar_tensor_tensor(out=XS[:, 2, :], in0=XS[:, 2, :], scalar=col(layer, "a_kv"), in1=RSTD["A"][1],
                                         op0=ALU.mult, op1=ALU.mult).then_inc(normed.sem, 1)
                rope(KR, 1, ROT["A"], A_ROPE, src=misc)
                dve.wait_ge(roped.sem, w.next(roped))
                done(dve.tensor_copy(KR[0:A_ROPE, SEQ:T], misc[0:A_ROPE, SEQ:T]))
                dve.tensor_copy(KR[A_ROPE:P, :], KR[0:A_ROPE, :]).then_inc(roped.sem, 1)
                dve.wait_ge(roped.sem, w.next(roped))
                for j in range(2):
                    rope(QR[:, j, :], 1 + 2 * j, ROT["A"])
                    dve.wait_ge(roped.sem, w.next(roped))

            def attention(branch, layer):
                tiles = attention_tiles(branch, layer)
                for i in range(len(tiles) + LAG + 2):
                    if i < len(tiles):
                        tile = tiles[i]
                        a, b = score_span(branch, tile)
                        s = i % 4
                        dve.wait_ge(scores_done.sem, w.next(scores_done))
                        done(dve.reduce_max(rowmax[:, s:s + 1], slot[i % 2][:, a:b], axis=AX.X))
                        if branch == "B":
                            head = tile["g"] * B_GROUP + tile["j"]
                            ins = dve.tensor_scalar(negmax[:, s:s + 1], rowmax[:, s:s + 1], -SCALE[branch], nsink[:, head:head + 1], ALU.mult, ALU.min)
                        else:
                            ins = dve.tensor_scalar(negmax[:, s:s + 1], rowmax[:, s:s + 1], -SCALE[branch], None, ALU.mult)
                        ins.then_inc(max_ready.sem, 1)
                    if 1 <= i <= len(tiles):
                        tile = tiles[i - 1]
                        a, b = score_span(branch, tile)
                        s = (i - 1) % 4
                        dve.wait_ge(exp_ready.sem, w.next(exp_ready))
                        if branch == "B":
                            done(dve.tensor_tensor(sums[:, s:s + 1], sums[:, s:s + 1], sink_e[:, s:s + 1], ALU.add))
                        done(dve.reciprocal(recip[:, s:s + 1], sums[:, s:s + 1]))
                        pb = PB[branch][(i - 1) % (LAG + 1)][:, 0:b - a]
                        dve.tensor_scalar(pb, pb, recip[:, s:s + 1], None, ALU.mult).then_inc(prob_ready.sem, 1)
                    if i - 1 > LAG and tiles[i - LAG - 2]["last"]:
                        dve.wait_ge(y_high.sem, w.next(y_high))
                        for (lo_, ps), (hi_, _) in zip(output_parts(branch, tiles[i - LAG - 2], Yl), output_parts(branch, tiles[i - LAG - 2], Yh)):
                            ins = dve.tensor_tensor(lo_, ps, hi_.bitcast(f32), ALU.subtract)
                        ins.then_inc(y_low.sem, 1)

            def modulation_columns(first, n):
                dve.wait_ge(mod_done.sem, w.next(mod_done))
                dve.tensor_copy(mod[:, first:first + n, :], slot[3][:, 0:2 * n].rearrange("p (a s) -> p a s", s=2)).then_inc(mod_read.sem, 1)
                dve.wait_ge(mod_read.sem, w.next(mod_read))

            def modulation_ready(layer, first, end, gain, name, scale_at):
                bias = cols[:, layer, COL["ada_b"] + first:COL["ada_b"] + end].unsqueeze(2).to_broadcast([P, end - first, 2])
                done(dve.tensor_tensor(mod[:, first:end, :], mod[:, first:end, :], bias, ALU.add))
                done(dve.tensor_scalar_add(gain[:, :, :], mod[:, scale_at:scale_at + KT, :], 1.0))
                nw = cols[:, layer, COL[name]:COL[name] + KT].unsqueeze(2).to_broadcast([P, KT, 2])
                dve.tensor_tensor(gain[:, :, :], gain[:, :, :], nw, ALU.mult).then_inc(gain_ready.sem, 1)

            def gates(branch, nq):
                n = jobs[0] % N_JOBS

                def gate_job(x, row, last):
                    p = (n + x) % 2
                    if not last or n + x + 1 < N_JOBS:
                        low(n + x + 1)
                    dve.wait_ge(gate_read.sem, w.next(gate_read))
                    dve.wait_ge(job_done.sem, w.next(job_done))
                    g, z = tmp[:, p, 0:nq], slot[2 * p + 1][:, 0:nq]
                    m = M[:, bass.ds(row, 1), 0:nq]
                    if branch == BRANCHES[0]:
                        dve.tensor_tensor(m, flat1(g), flat1(z), ALU.mult).then_inc(z_read.sem, 1)
                    else:
                        t = tmp[:, 2 + p, 0:nq]
                        dve.tensor_tensor(t, g, z, ALU.mult).then_inc(z_read.sem, 1)
                        dve.wait_ge(z_read.sem, w.next(z_read))
                        dve.tensor_tensor(m, m, flat1(t), ALU.add).then_inc(merged.sem, 1)
                        dve.wait_ge(merged.sem, w.next(merged))

                with w.loop(KT // 2 - 1, 2) as turn:
                    for x in range(2):
                        gate_job(x, turn * 2 + x, False)
                for x in range(KT - 2, KT):
                    gate_job(x, x, True)
                if branch == BRANCHES[0]:
                    dve.wait_ge(z_read.sem, w.next(z_read, KT))
                jobs[0] += KT

            def mlp(nq, ada):
                n = jobs[0] % N_JOBS

                def group(first_tile, final):
                    def hidden_low(p, j):
                        dve.wait_ge(u_high.sem, w.next(u_high))
                        dve.tensor_tensor(Ul[:, j, 0:nq], tmp[:, 2 + p, 0:nq], Uh[:, j, 0:nq].bitcast(f32), ALU.subtract).then_inc(u_low.sem, 1)
                        dve.wait_ge(u_low.sem, w.next(u_low))

                    for x in range(2 * KT):
                        p = (n + x) % 2
                        if not (final and x == 2 * KT - 1):
                            dve.wait_ge(high_done.sem, w.next(high_done))
                            q = 1 - p
                            dve.tensor_tensor(wl[q][:, 0:KT, :], raw[q][:, 0:KT, :], wh[q][:, 0:KT, :].bitcast(f32), ALU.subtract).then_inc(low_done.sem, 1)
                        if 0 < x <= KT:
                            hidden_low(1 - p, x - 1)
                        if final and x > KT:
                            add_squares(x - KT - 1, nq)
                        dve.wait_ge(job_done.sem, w.next(job_done))
                        if x < KT:
                            dve.wait_ge(relu_ready.sem, w.next(relu_ready))
                            if ada and x in ADA_STEPS:
                                dve.tensor_copy(mod_first_t[0:2, bass.ds(first_tile * P + ADA_STEPS.index(x) * P, P)], slot[2 * p][0:2, T:T + P])
                            dve.tensor_tensor(tmp[:, 2 + p, 0:nq], slot[2 * p][:, 0:nq], tmp[:, p, 0:nq], ALU.mult).then_inc(ff_read.sem, 1)
                        if x >= KT:
                            add_to_x(x - KT, 2 * p, MOD_GATE2, nq).then_inc(ff_read.sem, 1)
                    dve.wait_ge(ff_read.sem, w.next(ff_read, 2 * KT))
                    if final:
                        add_squares(KT - 1, nq)

                with w.loop(FF_GROUPS - 1, 2 * KT) as turn:
                    group(turn * ADA_PER_GROUP, False)
                group(ADA_PER_GROUP * (FF_GROUPS - 1), True)
                jobs[0] += 2 * KT * FF_GROUPS

            def add_to_x(k, where, gate_at, n):
                for lo, hi, side in sides(n):
                    ins = dve.scalar_tensor_tensor(out=X[:, k, lo:hi], in0=slot[where][:, lo:hi], scalar=mod[:, gate_at + k, side:side + 1],
                                                   in1=X[:, k, lo:hi], op0=ALU.mult, op1=ALU.add)
                return ins

            for n_, s_ in enumerate((gate_read, z_read, ff_read)):
                dve.memset(rowmax[:, n_:n_ + 1], 0.0).then_inc(s_.sem, s_.credit)
            dve.memset(epsc[:, :], EPS)
            dve.memset(ones[:, :], 1.0).then_inc(init_done.sem, 1)
            dve.wait_ge(consts_in.sem, w.next(consts_in, 5))
            dve.wait_ge(init_done.sem, w.next(init_done))
            dve.wait_ge(silu_e.sem, w.next(silu_e))
            done(dve.tensor_scalar_add(cs[:, :], cs[:, :], 1.0))
            done(dve.reciprocal(cs[:, :], cs[:, :]))
            dve.tensor_tensor(cs[:, :], cs[:, :], cv[:, :], ALU.mult).then_inc(cs_ready.sem, 1)
            for layer in range(DEPTH):
                nq = queries(layer)
                if layer == 0:
                    for k in range(KT):
                        add_squares(k, T)
                    for k in range(2):
                        dve.wait_ge(ada_read.sem, w.next(ada_read, ADA_FIRST // 2))
                        half = ADA_FIRST // 2 * P
                        dve.tensor_copy(mod_first_t[0:2, k * half:(k + 1) * half], slot[2 + k][0:2, 0:half]).then_inc(mod_t_ready.sem, 1)
                modulation_columns(0, ADA_FIRST)
                modulation_ready(layer, 0, ADA_FIRST, gain1, "norm1", MOD_SCALE1)
                dve.tensor_scalar(nsink[:, :], cols[:, layer, COL["sink"]:COL["sink"] + B_HEADS], -1.0, None, ALU.mult).then_inc(nsink_ready.sem, 1)
                if layer == 0:
                    dve.wait_ge(x_in.sem, w.next(x_in))
                low(0)
                norm(T, gain1, layer)
                dve.wait_ge(nsink_ready.sem, w.next(nsink_ready))
                for b in BRANCHES:
                    if b in "BD":
                        dve.wait_ge(tab_in.sem, w.next(tab_in))
                    project(b, layer, nq)
                    if b == "C":
                        branch_c(layer, nq)
                    if b in "CA":
                        dve.wait_ge(tab_in.sem, w.next(tab_in))
                    if b == "A":
                        branch_a(layer, nq)
                    if b != "C":
                        attention(b, layer)
                    gates(b, nq)
                for k in range(KT):
                    dve.wait_ge(m_high.sem, w.next(m_high))
                    dve.tensor_tensor(Ml[:, k, 0:nq], M[:, k, 0:nq], Mh[:, k, 0:nq].bitcast(f32), ALU.subtract).then_inc(m_low.sem, 1)
                dve.wait_ge(x_in.sem, w.next(x_in))
                for k in range(KT):
                    p = begin_job((k - 1, nq) if k else None)
                    if k == 0:
                        modulation_ready(layer, ADA_FIRST, ADA_TILES, gain2, "norm2", MOD_SCALE2)
                    add_to_x(k, 2 * p, MOD_GATE1, nq).then_inc(x_updated.sem, 1)
                dve.wait_ge(x_updated.sem, w.next(x_updated, KT))
                add_squares(KT - 1, nq)
                norm(nq, gain2, layer)
                mlp(nq, layer < DEPTH - 1)
            norm(SEQ, None, DEPTH - 1)


def tiles_of(w, cols):
    k = w.shape[0]
    return np.ascontiguousarray(w[:, cols].reshape(k // P, P, len(cols) // P, P).transpose(2, 1, 0, 3))


def rope_table(dim):
    half, quarter = dim // 2, dim // 4
    t = np.arange(SEQ)
    inv = (ROPE_BASE ** (-np.arange(quarter, dtype=np.float32) / quarter)).astype(np.float32)
    cos, sin, rot = np.zeros((P, SEQ), np.float32), np.zeros((P, SEQ), np.float32), np.zeros((P, P), np.float32)
    for p in range(P):
        f = p % dim
        pos = (t // GRID_W if f < half else t % GRID_W).astype(np.float32)
        ang = pos * inv[f % quarter]
        cos[p], sin[p] = np.cos(ang), np.sin(ang)
        if f % half < quarter:
            rot[p + quarter, p] = -1.0
        else:
            rot[p - quarter, p] = 1.0
    return np.concatenate([cos, sin, rot], axis=1)


def kernel(x, c, ctx, c_ctx, ada_w, ada_b, norm1_w, norm2_w, w_in, mla_q_norm_w, mla_w_uq, mla_kv_norm_w, mla_w_ukv,
           swa_sink, gla_w_decay, gla_b_decay, gla_norm_w, gqa_q_norm_w, gqa_k_norm_w, w_branch, w_o, mlp_w1, mlp_w2,
           final_norm_w):
    import concourse.bacc as bacc
    from concourse.bass_utils import run_bass_kernel_spmd

    (x, c, ctx, c_ctx, ada_w, ada_b, norm1_w, norm2_w, w_in, mla_q_norm_w, mla_w_uq, mla_kv_norm_w, mla_w_ukv, swa_sink,
     gla_w_decay, gla_b_decay, gla_norm_w, gqa_q_norm_w, gqa_k_norm_w, w_branch, w_o, mlp_w1, mlp_w2, final_norm_w) = [
        np.asarray(a) for a in (x, c, ctx, c_ctx, ada_w, ada_b, norm1_w, norm2_w, w_in, mla_q_norm_w, mla_w_uq,
                                mla_kv_norm_w, mla_w_ukv, swa_sink, gla_w_decay, gla_b_decay, gla_norm_w, gqa_q_norm_w,
                                gqa_k_norm_w, w_branch, w_o, mlp_w1, mlp_w2, final_norm_w)]
    feature_major = lambda a: np.ascontiguousarray(a.reshape(-1, KT, P).transpose(2, 1, 0))
    span = lambda start, n: np.arange(start, start + n)
    ada, w8, w12, cols, small, wdec = [], [], [], [], [], []
    for l in range(DEPTH):
        ada.append(tiles_of(ada_w[l], span(0, 6 * D_MODEL)))
        zero = np.zeros((D_MODEL, P - A_ROPE - 2 * C_RANK), np.float32)
        misc = np.concatenate([w_in[l][:, span(A0 + A_Q_RANK + A_KV_RANK, A_ROPE)], w_in[l][:, span(C_LR, 2 * C_RANK)], zero], 1)
        w8 += [tiles_of(w_in[l], span(C_R, 512)), tiles_of(misc, span(0, P)), tiles_of(w_in[l], span(C_Q, 256)),
               tiles_of(w_in[l], span(C_K, 256)), tiles_of(w_in[l], span(C_V, 512))]
        w8.append(tiles_of(w_in[l], span(A0, A_Q_RANK + A_KV_RANK)))
        heads = [g * B_GROUP + j for j in range(B_GROUP) for g in range(B_KV)]
        w8.append(tiles_of(w_in[l], np.concatenate([span(B0 + h * B_HD, B_HD) for h in heads])))
        w8.append(tiles_of(w_in[l], span(B0 + B_HEADS * B_HD, 2 * B_KV * B_HD)))
        w8.append(tiles_of(w_in[l], span(D0, (D_HEADS + 2 * D_KV) * D_HD)))
        w8.append(tiles_of(w_o[l], span(0, D_MODEL)))
        for g in range(FF_GROUPS):
            w8.append(tiles_of(mlp_w1[l], span(g * D_MODEL, D_MODEL)))
            w8.append(tiles_of(mlp_w2[l][g * D_MODEL:(g + 1) * D_MODEL], span(0, D_MODEL)))
        for b in BRANCHES:
            i = BRANCH_INDEX[b]
            gate = tiles_of(w_in[l], span(G0 + i * D_MODEL, D_MODEL))
            w12.append(np.concatenate([gate, tiles_of(w_branch[l, i], span(0, D_MODEL))], axis=2))
        per = lambda a: a.reshape(-1, P).T
        decay_bias = np.stack([np.concatenate([gla_b_decay[l, d, h * C_DK:(h + 1) * C_DK] for d in range(2)]) for h in range(C_HEADS)], 1)
        cols.append(np.concatenate([per(ada_b[l]), per(norm1_w[l]), per(norm2_w[l]), per(final_norm_w), per(mla_q_norm_w[l]),
                                    per(mla_kv_norm_w[l]), per(gla_norm_w[l]), per(gqa_q_norm_w[l]), per(gqa_k_norm_w[l]),
                                    decay_bias, np.broadcast_to(swa_sink[l], (P, B_HEADS))], axis=1))
        uq = mla_w_uq[l].reshape(2, P, A_HEADS, A_NOPE + A_ROPE)
        uq = np.concatenate([uq[..., :A_NOPE].reshape(2, P, -1), uq[..., A_NOPE:].reshape(2, P, -1)], axis=2).transpose(1, 0, 2)
        ukv = mla_w_ukv[l].reshape(P, A_HEADS, 2, P).transpose(0, 2, 1, 3)
        small.append(np.concatenate([uq.reshape(P, -1), ukv.reshape(P, -1)], axis=1))
        wd = np.zeros((2, C_RANK, C_HEADS, 2, C_DK), np.float32)
        for d in range(2):
            wd[d, :, :, d, :] = gla_w_decay[l, d].reshape(C_RANK, C_HEADS, C_DK)
        wdec.append(wd.reshape(2 * C_RANK, C_HEADS * P))
    s, t = np.arange(P)[:, None, None], np.arange(P)[None, None, :]
    halves = np.array(LEVELS[1:])[None, :, None]
    mask = (s // (2 * halves) == t // (2 * halves)) & (s // halves != t // halves)
    mask = np.concatenate([mask, s == t], axis=1).astype(np.float32)
    win = np.stack([np.where(t[:, 0] >= s[:, 0], 0.0, NEG_INF), np.where(t[:, 0] <= s[:, 0], 0.0, NEG_INF)], 1).astype(np.float32)
    arrays = {
        "ada": np.concatenate(ada),
        "w8": np.concatenate(w8), "w12": np.concatenate(w12),
        "xT": feature_major(np.concatenate([x[0], ctx[0]], axis=0)),
        "cvec": feature_major(np.stack([c[0], c_ctx])).reshape(P, 2 * KT),
        "cols": np.ascontiguousarray(np.stack(cols, axis=1)), "small": np.stack(small), "wdec": np.stack(wdec),
        "tabs": np.stack([rope_table(A_ROPE), rope_table(D_HD)]), "ident": np.eye(P, dtype=np.float32),
        "glamask": mask, "winmask": win,
    }
    nc = bacc.Bacc("TRN2", target_bir_lowering=False, num_devices=1)
    aps = [nc.dram_tensor(f"{n}_dram", a.shape, mybir.dt.from_np(a.dtype), kind="ExternalInput").ap() for n, a in arrays.items()]
    out = nc.dram_tensor("out_dram", (P, KT, SEQ), mybir.dt.float32, kind="ExternalOutput").ap()
    build(nc, *aps, out)
    r = run_bass_kernel_spmd(nc, [{f"{n}_dram": a for n, a in arrays.items()}], core_ids=[0])
    y = r.results[0]["out_dram"]
    return np.ascontiguousarray(y.transpose(2, 1, 0).reshape(1, SEQ, D_MODEL))
```
